# Optimizing a Trainium2 kernel written in Bass

```python
import math
import jax, jax.numpy as jnp
from jax import lax
import numpy as np

D_MODEL = 1024
BATCH = 1
SEQ = 512
DEPTH = 1

HEAD_DIM = 64
ROPE_DIMS = HEAD_DIM // 4
ROPE_THETA = 500000.0
NORM_EPS = 1e-6
NEG_INF = -1e30

NSA_HEADS = 8
NSA_KV_GROUPS = 2
NSA_Q_PER_KV = NSA_HEADS // NSA_KV_GROUPS
CMP_BLOCK = 32
CMP_STRIDE = 16
CMP_HIDDEN = 256
SLC_BLOCK = 64
SLC_TOPN = 16
FORCE_SCORE = 1e3
WIN = 512
NSA_QBLOCK = 64

DIL_PATTERNS = ((128, 1), (512, 4), (2048, 16))
DIL_GROUPS = len(DIL_PATTERNS)
DIL_HEADS_PER_GROUP = 4
DIL_WIDTH = DIL_HEADS_PER_GROUP * HEAD_DIM
DIL_BLOCK = 128

NSA_Q_COLS = NSA_HEADS * HEAD_DIM
NSA_KV_COLS = NSA_KV_GROUPS * HEAD_DIM
NSA_GATE_COLS = 3 * NSA_HEADS
DIL_COLS = DIL_GROUPS * 3 * DIL_WIDTH
MERGE_COLS = 2 * D_MODEL
IN_COLS = NSA_Q_COLS + 6 * NSA_KV_COLS + NSA_GATE_COLS + DIL_COLS + MERGE_COLS

PEER_HEADS = 8
PEER_NKEYS = 128
PEER_TOPK = 16
PEER_QDIM = 128
PEER_N_EXPERTS = PEER_NKEYS ** 2
PEER_CHUNK = 128


def rms_norm(z, g):
    zf = z.astype(jnp.float32)
    zf = zf * lax.rsqrt(jnp.mean(zf * zf, axis=-1, keepdims=True) + NORM_EPS)
    return (zf * g.astype(jnp.float32)).astype(z.dtype)

def rope(z, pos):
    half = ROPE_DIMS // 2
    inv = ROPE_THETA ** (-(jnp.arange(half, dtype=jnp.float32) * 2.0 / ROPE_DIMS))
    ang = pos.astype(jnp.float32)[:, None] * inv[None, :]
    cos = jnp.cos(ang)[None, :, None, :]
    sin = jnp.sin(ang)[None, :, None, :]
    zf = z.astype(jnp.float32)
    z1 = zf[..., :half]
    z2 = zf[..., half:ROPE_DIMS]
    out = jnp.concatenate([z1 * cos - z2 * sin, z1 * sin + z2 * cos, zf[..., ROPE_DIMS:]], axis=-1)
    return out.astype(z.dtype)

def compress_blocks(z, idx, pe, w1, w2):
    B, _, G, dh = z.shape
    blk = z[:, idx] + pe[None, None, :, None, :]
    n_cmp = idx.shape[0]
    flat = blk.transpose(0, 1, 3, 2, 4).reshape(B, n_cmp, G, CMP_BLOCK * dh)
    return jax.nn.gelu(flat @ w1) @ w2

def nsa_attention(q, k_c, v_c, k_s, v_s, k_w, v_w, gate_logits, q_norm, k_norm,
                  cmp_pe_k, cmp_w1_k, cmp_w2_k, cmp_pe_v, cmp_w1_v, cmp_w2_v):
    B, S, _ = q.shape
    G, HG, dh = NSA_KV_GROUPS, NSA_Q_PER_KV, HEAD_DIM
    scale = HEAD_DIM ** -0.5
    dtype = q.dtype
    pos = jnp.arange(S, dtype=jnp.int32)
    q = rope(rms_norm(q.reshape(B, S, NSA_HEADS, dh), q_norm), pos)
    shp = (B, S, G, dh)
    k_s = rope(rms_norm(k_s.reshape(shp), k_norm[1]), pos)
    k_w = rope(rms_norm(k_w.reshape(shp), k_norm[2]), pos)
    v_s = v_s.reshape(shp)
    v_w = v_w.reshape(shp)

    n_cmp = (S - CMP_BLOCK) // CMP_STRIDE + 1
    starts = jnp.arange(n_cmp, dtype=jnp.int32) * CMP_STRIDE
    idx = starts[:, None] + jnp.arange(CMP_BLOCK, dtype=jnp.int32)[None, :]
    cmp_end = starts + CMP_BLOCK - 1
    k_cmp = compress_blocks(k_c.reshape(shp), idx, cmp_pe_k, cmp_w1_k, cmp_w2_k)
    v_cmp = compress_blocks(v_c.reshape(shp), idx, cmp_pe_v, cmp_w1_v, cmp_w2_v)
    k_cmp = rope(rms_norm(k_cmp, k_norm[0]), cmp_end)

    n_slc = S // SLC_BLOCK
    n_sel = min(SLC_TOPN, n_slc)
    s0 = np.arange(n_cmp) * CMP_STRIDE
    s1 = s0 + CMP_BLOCK
    b0 = np.arange(n_slc) * SLC_BLOCK
    b1 = b0 + SLC_BLOCK
    ov = np.clip(np.minimum(s1[:, None], b1[None, :]) - np.maximum(s0[:, None], b0[None, :]), 0, None) / CMP_BLOCK
    overlap = jnp.asarray(ov, dtype=jnp.float32)

    ks_blk = k_s.reshape(B, n_slc, SLC_BLOCK, G, dh).transpose(0, 3, 1, 2, 4)
    vs_blk = v_s.reshape(B, n_slc, SLC_BLOCK, G, dh).transpose(0, 3, 1, 2, 4)
    kw_pad = jnp.pad(k_w, ((0, 0), (WIN, 0), (0, 0), (0, 0)))
    vw_pad = jnp.pad(v_w, ((0, 0), (WIN, 0), (0, 0), (0, 0)))
    gates = jax.nn.sigmoid(gate_logits.astype(jnp.float32)).reshape(B, S, NSA_HEADS, 3)
    bi = jnp.arange(B)[:, None, None, None]
    gi = jnp.arange(G)[None, :, None, None]
    blk_ids = jnp.arange(n_slc, dtype=jnp.int32)
    QB = NSA_QBLOCK

    def body(n):
        t0 = n * QB
        t = t0 + jnp.arange(QB, dtype=jnp.int32)
        qb = lax.dynamic_slice_in_dim(q, t0, QB, axis=1).reshape(B, QB, G, HG, dh)
        sc = jnp.einsum('bqgjd,bcgd->bgjqc', qb, k_cmp).astype(jnp.float32) * scale
        valid_c = cmp_end[None, :] <= t[:, None]
        pc = jax.nn.softmax(jnp.where(valid_c, sc, NEG_INF), axis=-1)
        pc = jnp.where(valid_c, pc, 0.0)
        o_c = jnp.einsum('bgjqc,bcgd->bqgjd', pc.astype(dtype), v_cmp)
        imp = jnp.einsum('bgjqc,cn->bgqn', pc, overlap)
        cur = t // SLC_BLOCK
        forced = (blk_ids[None, :] == 0) | (blk_ids[None, :] == cur[:, None]) | (blk_ids[None, :] == cur[:, None] - 1)
        causal_b = blk_ids[None, :] * SLC_BLOCK <= t[:, None]
        score = jnp.where(forced, FORCE_SCORE, jnp.where(causal_b, imp, -1.0))
        _, sel = lax.top_k(score, n_sel)
        kg = ks_blk[bi, gi, sel]
        vg = vs_blk[bi, gi, sel]
        ss = jnp.einsum('bqgjd,bgqnkd->bgjqnk', qb, kg).astype(jnp.float32) * scale
        kpos = sel[..., None] * SLC_BLOCK + jnp.arange(SLC_BLOCK, dtype=jnp.int32)
        valid_s = kpos <= t[None, None, :, None, None]
        ss = jnp.where(valid_s[:, :, None], ss, NEG_INF).reshape(B, G, HG, QB, n_sel * SLC_BLOCK)
        ps = jax.nn.softmax(ss, axis=-1).reshape(B, G, HG, QB, n_sel, SLC_BLOCK)
        o_s = jnp.einsum('bgjqnk,bgqnkd->bqgjd', ps.astype(dtype), vg)
        kwb = lax.dynamic_slice_in_dim(kw_pad, t0, QB + WIN, axis=1)
        vwb = lax.dynamic_slice_in_dim(vw_pad, t0, QB + WIN, axis=1)
        kp = t0 - WIN + jnp.arange(QB + WIN, dtype=jnp.int32)
        dist = t[:, None] - kp[None, :]
        valid_w = (dist >= 0) & (dist < WIN) & (kp[None, :] >= 0)
        sw = jnp.einsum('bqgjd,bkgd->bgjqk', qb, kwb).astype(jnp.float32) * scale
        pw = jax.nn.softmax(jnp.where(valid_w, sw, NEG_INF), axis=-1)
        o_w = jnp.einsum('bgjqk,bkgd->bqgjd', pw.astype(dtype), vwb)
        gb = lax.dynamic_slice_in_dim(gates, t0, QB, axis=1).reshape(B, QB, G, HG, 3)
        o = gb[..., 0:1] * o_c + gb[..., 1:2] * o_s + gb[..., 2:3] * o_w
        return o.reshape(B, QB, NSA_HEADS * dh).astype(dtype)

    out = lax.map(body, jnp.arange(S // QB, dtype=jnp.int32))
    return out.transpose(1, 0, 2, 3).reshape(B, S, NSA_HEADS * dh)

def dilated_group(q, k, v, window, dilation):
    B, S, H, dh = q.shape
    scale = HEAD_DIM ** -0.5
    n_back = window // dilation
    L = -(-S // dilation)
    L = -(-L // DIL_BLOCK) * DIL_BLOCK
    Sp = L * dilation
    nb = L // DIL_BLOCK
    pad = ((0, 0), (0, Sp - S), (0, 0), (0, 0))

    def to_blocks(z):
        z = jnp.pad(z, pad).reshape(B, L, dilation, H, dh).transpose(0, 2, 3, 1, 4)
        return z.reshape(B, dilation, H, nb, DIL_BLOCK, dh)

    def with_prev(z):
        prev = jnp.pad(z[:, :, :, :-1], ((0, 0), (0, 0), (0, 0), (1, 0), (0, 0), (0, 0)))
        return jnp.concatenate([prev, z], axis=4)

    qb = to_blocks(q)
    kk = with_prev(to_blocks(k))
    vv = with_prev(to_blocks(v))
    s = jnp.einsum('brhnqd,brhnkd->brhnqk', qb, kk).astype(jnp.float32) * scale
    blk = jnp.arange(nb, dtype=jnp.int32)[:, None]
    pq = blk * DIL_BLOCK + jnp.arange(DIL_BLOCK, dtype=jnp.int32)[None, :]
    pk = (blk - 1) * DIL_BLOCK + jnp.arange(2 * DIL_BLOCK, dtype=jnp.int32)[None, :]
    dist = pq[:, :, None] - pk[:, None, :]
    valid = (dist >= 0) & (dist <= n_back) & (pk[:, None, :] >= 0)
    s = jnp.where(valid, s, NEG_INF)
    m = jnp.max(s, axis=-1, keepdims=True)
    e = jnp.exp(s - m)
    den = jnp.sum(e, axis=-1)
    o = jnp.einsum('brhnqk,brhnkd->brhnqd', e, vv.astype(jnp.float32)) / den[..., None]
    lse = m[..., 0] + jnp.log(den)
    o = o.reshape(B, dilation, H, L, dh).transpose(0, 3, 1, 2, 4).reshape(B, Sp, H, dh)[:, :S]
    lse = lse.reshape(B, dilation, H, L).transpose(0, 3, 1, 2).reshape(B, Sp, H)[:, :S]
    return o, lse

def dilated_attention(d_cols, q_norm, k_norm):
    B, S, _ = d_cols.shape
    pos = jnp.arange(S, dtype=jnp.int32)
    d = d_cols.reshape(B, S, DIL_GROUPS, 3, DIL_HEADS_PER_GROUP, HEAD_DIM)
    outs, lses = [], []
    for g, (window, dilation) in enumerate(DIL_PATTERNS):
        qg = rope(rms_norm(d[:, :, g, 0], q_norm[g]), pos)
        kg = rope(rms_norm(d[:, :, g, 1], k_norm[g]), pos)
        o, lse = dilated_group(qg, kg, d[:, :, g, 2], window, dilation)
        outs.append(o)
        lses.append(lse)
    alpha = jax.nn.softmax(jnp.stack(lses, axis=0), axis=0)
    o = jnp.sum(alpha[..., None] * jnp.stack(outs, axis=0), axis=0)
    return o.reshape(B, S, DIL_WIDTH).astype(d_cols.dtype)

def peer(hn, w_q, subkeys, u, v):
    B, S, D = hn.shape
    T = B * S
    H, K = PEER_HEADS, PEER_TOPK
    xt = hn.reshape(T, D)
    q = (xt @ w_q).reshape(T, H, 2, PEER_QDIM // 2)
    s = jnp.einsum('thcd,cnd->thcn', q, subkeys).astype(jnp.float32)
    s1, i1 = lax.top_k(s[:, :, 0], K)
    s2, i2 = lax.top_k(s[:, :, 1], K)
    cand = (s1[..., :, None] + s2[..., None, :]).reshape(T, H, K * K)
    sc, ci = lax.top_k(cand, K)
    e1 = jnp.take_along_axis(i1, ci // K, axis=-1)
    e2 = jnp.take_along_axis(i2, ci % K, axis=-1)
    idx = e1 * PEER_NKEYS + e2
    g = jax.nn.softmax(sc, axis=-1)
    C = PEER_CHUNK
    nc = T // C

    def body(args):
        xc, ic, gc = args
        a = jnp.einsum('cd,chkd->chk', xc, u[ic])
        act = (jax.nn.gelu(a.astype(jnp.float32)) * gc).astype(xc.dtype)
        return jnp.einsum('chk,chkd->cd', act, v[ic])

    out = lax.map(body, (xt.reshape(nc, C, D), idx.reshape(nc, C, H, K), g.reshape(nc, C, H, K)))
    return out.reshape(B, S, D)

def first_inputs(seed: int = 0) -> dict:
    key = jax.random.key(seed)
    ks = jax.random.split(key, 24)
    f32 = jnp.float32

    def nrm(k, shape, scale):
        return jax.random.normal(k, shape, f32) * scale

    def gain(k, shape):
        return 1.0 + 0.02 * jax.random.normal(k, shape, f32)

    flat = CMP_BLOCK * HEAD_DIM
    nsa_w = NSA_HEADS * HEAD_DIM
    return {
        "x": nrm(ks[0], (BATCH, SEQ, D_MODEL), 1.0),
        "norm1_g": gain(ks[1], (D_MODEL,)),
        "w_in": nrm(ks[2], (D_MODEL, IN_COLS), D_MODEL ** -0.5),
        "nsa_q_norm": gain(ks[3], (HEAD_DIM,)),
        "nsa_k_norm": gain(ks[4], (3, HEAD_DIM)),
        "cmp_pe_k": nrm(ks[5], (CMP_BLOCK, HEAD_DIM), 0.1),
        "cmp_w1_k": nrm(ks[6], (flat, CMP_HIDDEN), flat ** -0.5),
        "cmp_w2_k": nrm(ks[7], (CMP_HIDDEN, HEAD_DIM), CMP_HIDDEN ** -0.5),
        "cmp_pe_v": nrm(ks[8], (CMP_BLOCK, HEAD_DIM), 0.1),
        "cmp_w1_v": nrm(ks[9], (flat, CMP_HIDDEN), flat ** -0.5),
        "cmp_w2_v": nrm(ks[10], (CMP_HIDDEN, HEAD_DIM), CMP_HIDDEN ** -0.5),
        "dil_q_norm": gain(ks[11], (DIL_GROUPS, HEAD_DIM)),
        "dil_k_norm": gain(ks[12], (DIL_GROUPS, HEAD_DIM)),
        "w_up_nsa": nrm(ks[13], (nsa_w, D_MODEL), nsa_w ** -0.5),
        "w_up_dil": nrm(ks[14], (DIL_WIDTH, D_MODEL), DIL_WIDTH ** -0.5),
        "w_o": nrm(ks[15], (D_MODEL, D_MODEL), D_MODEL ** -0.5),
        "norm2_g": gain(ks[16], (D_MODEL,)),
        "peer_wq": nrm(ks[17], (D_MODEL, PEER_HEADS * PEER_QDIM), D_MODEL ** -0.5),
        "peer_subkeys": nrm(ks[18], (2, PEER_NKEYS, PEER_QDIM // 2), (PEER_QDIM // 2) ** -0.5),
        "peer_u": nrm(ks[19], (PEER_N_EXPERTS, D_MODEL), D_MODEL ** -0.5),
        "peer_v": nrm(ks[20], (PEER_N_EXPERTS, D_MODEL), PEER_HEADS ** -0.5),
    }

def first_block(x, norm1_g, w_in, nsa_q_norm, nsa_k_norm, cmp_pe_k, cmp_w1_k, cmp_w2_k,
              cmp_pe_v, cmp_w1_v, cmp_w2_v, dil_q_norm, dil_k_norm, w_up_nsa, w_up_dil,
              w_o, norm2_g, peer_wq, peer_subkeys, peer_u, peer_v):
    B, S, D = x.shape
    sizes = [NSA_Q_COLS] + [NSA_KV_COLS] * 6 + [NSA_GATE_COLS, DIL_COLS, MERGE_COLS]
    splits = [int(c) for c in np.cumsum(sizes)[:-1]]
    for _ in range(DEPTH):
        h = rms_norm(x, norm1_g)
        z = jnp.einsum('bsd,dc->bsc', h, w_in)
        q_n, kc, vc, ksl, vsl, kwn, vwn, g_nsa, dil, mg = jnp.split(z, splits, axis=-1)
        y_nsa = nsa_attention(q_n, kc, vc, ksl, vsl, kwn, vwn, g_nsa, nsa_q_norm, nsa_k_norm,
                              cmp_pe_k, cmp_w1_k, cmp_w2_k, cmp_pe_v, cmp_w1_v, cmp_w2_v)
        y_dil = dilated_attention(dil, dil_q_norm, dil_k_norm)
        gm = jax.nn.sigmoid(mg.astype(jnp.float32)).reshape(B, S, 2, D)
        merged = gm[:, :, 0] * (y_nsa @ w_up_nsa) + gm[:, :, 1] * (y_dil @ w_up_dil)
        x = x + merged.astype(x.dtype) @ w_o
        x = x + peer(rms_norm(x, norm2_g), peer_wq, peer_subkeys, peer_u, peer_v)
    return x


DEPTH_2 = 2

POOL_WIDTH = 512
POOL_WINDOWS = (2, 4, 8, 16)
POOL_GROUPS = len(POOL_WINDOWS)
POOL_GROUP_DIM = POOL_WIDTH // POOL_GROUPS
GLA_HEADS = 4
GLA_DK = 64
GLA_DV = 128
GLA_KEY_WIDTH = GLA_HEADS * GLA_DK
GLA_VAL_WIDTH = GLA_HEADS * GLA_DV
GLA_GATE_RANK = 16
GLA_GATE_TAU = 16.0
GLA_CHUNK = 64
MLA_HEADS = 8
MLA_Q_RANK = 384
MLA_KV_RANK = 256
MLA_NOPE = 64
MLA_ROPE = 32
MLA_V = 64
MLA_QK = MLA_NOPE + MLA_ROPE
MLA_VAL_WIDTH = MLA_HEADS * MLA_V
ROPE_BASE = 10000.0
Q_BLOCK = 128
N_BRANCH = 3
D_FF = -(-8 * D_MODEL // (3 * 256)) * 256
EPS = 1e-6

IN_SIZES = (POOL_WIDTH, GLA_KEY_WIDTH, GLA_KEY_WIDTH, GLA_VAL_WIDTH, GLA_VAL_WIDTH, GLA_GATE_RANK,
            MLA_Q_RANK, MLA_KV_RANK, MLA_ROPE, N_BRANCH * D_MODEL)
IN_WIDTH = sum(IN_SIZES)
IN_OFFSETS = tuple(int(v) for v in np.cumsum(IN_SIZES)[:-1])


def rms_norm_2(x, g):
    xf = x.astype(jnp.float32)
    y = xf * lax.rsqrt(jnp.mean(xf * xf, axis=-1, keepdims=True) + EPS)
    return (y * g.astype(jnp.float32)).astype(x.dtype)

def rope_tables(positions):
    inv_freq = ROPE_BASE ** (-jnp.arange(0, MLA_ROPE, 2, dtype=jnp.float32) / MLA_ROPE)
    ang = positions.astype(jnp.float32)[..., None] * inv_freq
    return jnp.cos(ang), jnp.sin(ang)

def apply_rope(x, cos, sin):
    half = x.shape[-1] // 2
    x1, x2 = x[..., :half], x[..., half:]
    return jnp.concatenate([x1 * cos - x2 * sin, x2 * cos + x1 * sin], axis=-1).astype(x.dtype)

def pool_mixer(u, w_pool, pool_scale):
    b, s, _ = u.shape
    uf = u.astype(jnp.float32).reshape(b, s, POOL_GROUPS, POOL_GROUP_DIM)
    cs = jnp.cumsum(uf, axis=1)
    t = jnp.arange(s)
    means = []
    for g, w in enumerate(POOL_WINDOWS):
        c = cs[:, :, g]
        prev = jnp.pad(c, ((0, 0), (w, 0), (0, 0)))[:, :s]
        cnt = jnp.minimum(t + 1, w).astype(jnp.float32)[None, :, None]
        means.append((c - prev) / cnt)
    pooled = jnp.stack(means, axis=2)
    diff = (pooled - uf).astype(u.dtype)
    y = jnp.einsum('bsgc,gcd->bsgd', diff, w_pool).reshape(b, s, POOL_WIDTH)
    return y * pool_scale

def gla_mixer(q, k, v, r, a1, w_a2, b_a, g_norm):
    b, s, _ = q.shape
    n = s // GLA_CHUNK
    f32 = jnp.float32
    log_a = jax.nn.log_sigmoid((a1 @ w_a2 + b_a).astype(f32)) / GLA_GATE_TAU

    def heads(t, d):
        return t.astype(f32).reshape(b, n, GLA_CHUNK, GLA_HEADS, d).transpose(0, 3, 1, 2, 4)

    qh = heads(q, GLA_DK) * (GLA_DK ** -0.5)
    kh = heads(k, GLA_DK)
    vh = heads(v, GLA_DV)
    cum = jnp.cumsum(heads(log_a, GLA_DK), axis=3)
    cum_last = cum[:, :, :, -1:, :]
    q_dec = qh * jnp.exp(cum)
    k_inv = kh * jnp.exp(-cum)
    k_end = kh * jnp.exp(cum_last - cum)
    mask = jnp.tril(jnp.ones((GLA_CHUNK, GLA_CHUNK), dtype=bool))
    att = jnp.where(mask, jnp.einsum('bhntd,bhnsd->bhnts', q_dec, k_inv), 0.0)
    o_intra = jnp.einsum('bhnts,bhnse->bhnte', att, vh)
    kv = jnp.einsum('bhnsd,bhnse->bhnde', k_end, vh)
    decay = jnp.exp(cum_last[:, :, :, 0, :])

    def step(state, inp):
        dec, kv_n = inp
        return dec[..., None] * state + kv_n, state

    s0 = jnp.zeros((b, GLA_HEADS, GLA_DK, GLA_DV), f32)
    _, states = lax.scan(step, s0, (jnp.moveaxis(decay, 2, 0), jnp.moveaxis(kv, 2, 0)))
    states = jnp.moveaxis(states, 0, 2)
    o_inter = jnp.einsum('bhntd,bhnde->bhnte', q_dec, states)
    o = (o_intra + o_inter).transpose(0, 2, 3, 1, 4).reshape(b, s, GLA_HEADS, GLA_DV)
    o = o * lax.rsqrt(jnp.mean(o * o, axis=-1, keepdims=True) + EPS)
    o = o * g_norm.astype(f32).reshape(GLA_HEADS, GLA_DV)
    o = o.reshape(b, s, GLA_VAL_WIDTH) * jax.nn.silu(r.astype(f32))
    return o.astype(q.dtype)

def mla_mixer(cq, ckv, kr, cos, sin, q_norm, w_uq, kv_norm, w_ukv):
    b, s, _ = cq.shape
    qf = (rms_norm_2(cq, q_norm) @ w_uq).reshape(b, s, MLA_HEADS, MLA_QK)
    kvf = (rms_norm_2(ckv, kv_norm) @ w_ukv).reshape(b, s, MLA_HEADS, MLA_NOPE + MLA_V)
    q_nope, q_rope = qf[..., :MLA_NOPE], qf[..., MLA_NOPE:]
    k_nope, v = kvf[..., :MLA_NOPE], kvf[..., MLA_NOPE:]
    q_rope = apply_rope(q_rope, cos[:, :, None], sin[:, :, None])
    k_rope = apply_rope(kr, cos, sin)
    q = jnp.concatenate([q_nope, q_rope], axis=-1)
    k = jnp.concatenate([k_nope, jnp.broadcast_to(k_rope[:, :, None], (b, s, MLA_HEADS, MLA_ROPE))], axis=-1)
    nb = s // Q_BLOCK
    qb = q.reshape(b, nb, Q_BLOCK, MLA_HEADS, MLA_QK).transpose(1, 0, 2, 3, 4)
    starts = jnp.arange(nb) * Q_BLOCK
    kpos = jnp.arange(s)
    scale = MLA_QK ** -0.5

    def attend(args):
        q_blk, start = args
        sc = jnp.einsum('bqhd,bkhd->bhqk', q_blk, k).astype(jnp.float32) * scale
        qpos = start + jnp.arange(Q_BLOCK)
        sc = jnp.where(qpos[:, None] >= kpos[None, :], sc, jnp.finfo(jnp.float32).min)
        p = jax.nn.softmax(sc, axis=-1)
        return jnp.einsum('bhqk,bkhe->bqhe', p.astype(v.dtype), v)

    o = lax.map(attend, (qb, starts))
    return o.transpose(1, 0, 2, 3, 4).reshape(b, s, MLA_VAL_WIDTH)

def hybrid_layer(x, cos, sin, n_pre_mix, n_post_mix, n_pre_ffn, n_post_ffn, w_in, w_pool, pool_scale, w_a,
                 w_gla_a2, b_gla_a, gla_norm, w_b, mla_q_norm, w_mla_uq, mla_kv_norm, w_mla_ukv, w_c, w_o,
                 w_ffn_gu, w_ffn_down):
    b, s, d = x.shape
    h = rms_norm_2(x, n_pre_mix)
    proj = h @ w_in
    (u_pool, g_q, g_k, g_v, g_r, g_a1, m_cq, m_ckv, m_kr, gate_logits) = jnp.split(proj, IN_OFFSETS, axis=-1)
    y_a = pool_mixer(u_pool, w_pool, pool_scale) @ w_a
    y_b = gla_mixer(g_q, g_k, g_v, g_r, g_a1, w_gla_a2, b_gla_a, gla_norm) @ w_b
    y_c = mla_mixer(m_cq, m_ckv, m_kr, cos, sin, mla_q_norm, w_mla_uq, mla_kv_norm, w_mla_ukv) @ w_c
    gates = jax.nn.sigmoid(gate_logits.astype(jnp.float32)).astype(x.dtype).reshape(b, s, N_BRANCH, d)
    merged = gates[:, :, 0] * y_a + gates[:, :, 1] * y_b + gates[:, :, 2] * y_c
    x = x + rms_norm_2(merged @ w_o, n_post_mix)
    h = rms_norm_2(x, n_pre_ffn)
    gu = h @ w_ffn_gu
    ffn = (jax.nn.silu(gu[..., :D_FF]) * gu[..., D_FF:]) @ w_ffn_down
    return x + rms_norm_2(ffn, n_post_ffn)

def second_inputs(seed: int = 0) -> dict:
    key = jax.random.key(seed)
    ks = jax.random.split(key, 24)
    f32 = jnp.float32

    def dense(k, shape, fan_in):
        return jax.random.normal(k, shape, f32) * (fan_in ** -0.5)

    def gain(k, shape):
        return 1.0 + 0.02 * jax.random.normal(k, shape, f32)

    x = jax.random.normal(ks[0], (BATCH, SEQ, D_MODEL), f32)
    offsets = jax.random.randint(ks[1], (BATCH, 1), 0, 4096, dtype=jnp.int32)
    positions = offsets + jnp.arange(SEQ, dtype=jnp.int32)[None, :]
    return {
        "x": x,
        "positions": positions,
        "norm_pre_mix": gain(ks[2], (DEPTH_2, D_MODEL)),
        "norm_post_mix": gain(ks[3], (DEPTH_2, D_MODEL)),
        "norm_pre_ffn": gain(ks[4], (DEPTH_2, D_MODEL)),
        "norm_post_ffn": gain(ks[5], (DEPTH_2, D_MODEL)),
        "w_in": dense(ks[6], (DEPTH_2, D_MODEL, IN_WIDTH), D_MODEL),
        "w_pool": dense(ks[7], (DEPTH_2, POOL_GROUPS, POOL_GROUP_DIM, POOL_GROUP_DIM), POOL_GROUP_DIM),
        "pool_scale": gain(ks[8], (DEPTH_2, POOL_WIDTH)),
        "w_a": dense(ks[9], (DEPTH_2, POOL_WIDTH, D_MODEL), POOL_WIDTH),
        "w_gla_a2": dense(ks[10], (DEPTH_2, GLA_GATE_RANK, GLA_KEY_WIDTH), GLA_GATE_RANK),
        "b_gla_a": 0.1 * jax.random.normal(ks[11], (DEPTH_2, GLA_KEY_WIDTH), f32),
        "gla_norm": gain(ks[12], (DEPTH_2, GLA_VAL_WIDTH)),
        "w_b": dense(ks[13], (DEPTH_2, GLA_VAL_WIDTH, D_MODEL), GLA_VAL_WIDTH),
        "mla_q_norm": gain(ks[14], (DEPTH_2, MLA_Q_RANK)),
        "w_mla_uq": dense(ks[15], (DEPTH_2, MLA_Q_RANK, MLA_HEADS * MLA_QK), MLA_Q_RANK),
        "mla_kv_norm": gain(ks[16], (DEPTH_2, MLA_KV_RANK)),
        "w_mla_ukv": dense(ks[17], (DEPTH_2, MLA_KV_RANK, MLA_HEADS * (MLA_NOPE + MLA_V)), MLA_KV_RANK),
        "w_c": dense(ks[18], (DEPTH_2, MLA_VAL_WIDTH, D_MODEL), MLA_VAL_WIDTH),
        "w_o": dense(ks[19], (DEPTH_2, D_MODEL, D_MODEL), D_MODEL),
        "w_ffn_gu": dense(ks[20], (DEPTH_2, D_MODEL, 2 * D_FF), D_MODEL),
        "w_ffn_down": dense(ks[21], (DEPTH_2, D_FF, D_MODEL), D_FF),
    }

def second_block(x, positions, norm_pre_mix, norm_post_mix, norm_pre_ffn, norm_post_ffn, w_in, w_pool,
              pool_scale, w_a, w_gla_a2, b_gla_a, gla_norm, w_b, mla_q_norm, w_mla_uq, mla_kv_norm,
              w_mla_ukv, w_c, w_o, w_ffn_gu, w_ffn_down):
    cos, sin = rope_tables(positions)
    for l in range(DEPTH_2):
        x = hybrid_layer(x, cos, sin, norm_pre_mix[l], norm_post_mix[l], norm_pre_ffn[l], norm_post_ffn[l],
                         w_in[l], w_pool[l], pool_scale[l], w_a[l], w_gla_a2[l], b_gla_a[l], gla_norm[l],
                         w_b[l], mla_q_norm[l], w_mla_uq[l], mla_kv_norm[l], w_mla_ukv[l], w_c[l], w_o[l],
                         w_ffn_gu[l], w_ffn_down[l])
    return x


def setup_inputs(seed=0):
    out = dict(first_inputs(seed))
    for name, value in second_inputs(seed + 1).items():
        if name != "x":
            out[name + "_2"] = value
    return out


def reference(
    x, norm1_g, w_in, nsa_q_norm, nsa_k_norm, cmp_pe_k, cmp_w1_k, cmp_w2_k, cmp_pe_v, cmp_w1_v,
    cmp_w2_v, dil_q_norm, dil_k_norm, w_up_nsa, w_up_dil, w_o, norm2_g, peer_wq, peer_subkeys,
    peer_u, peer_v, positions_2, norm_pre_mix_2, norm_post_mix_2, norm_pre_ffn_2,
    norm_post_ffn_2, w_in_2, w_pool_2, pool_scale_2, w_a_2, w_gla_a2_2, b_gla_a_2, gla_norm_2,
    w_b_2, mla_q_norm_2, w_mla_uq_2, mla_kv_norm_2, w_mla_ukv_2, w_c_2, w_o_2, w_ffn_gu_2,
    w_ffn_down_2,
):
    x = first_block(
        x, norm1_g, w_in, nsa_q_norm, nsa_k_norm, cmp_pe_k, cmp_w1_k, cmp_w2_k, cmp_pe_v,
        cmp_w1_v, cmp_w2_v, dil_q_norm, dil_k_norm, w_up_nsa, w_up_dil, w_o, norm2_g, peer_wq,
        peer_subkeys, peer_u, peer_v,
    )
    return second_block(
        x, positions_2, norm_pre_mix_2, norm_post_mix_2, norm_pre_ffn_2, norm_post_ffn_2,
        w_in_2, w_pool_2, pool_scale_2, w_a_2, w_gla_a2_2, b_gla_a_2, gla_norm_2, w_b_2,
        mla_q_norm_2, w_mla_uq_2, mla_kv_norm_2, w_mla_ukv_2, w_c_2, w_o_2, w_ffn_gu_2,
        w_ffn_down_2,
    )


_drawn_inputs = setup_inputs


def setup_inputs(seed=0):
    import zlib

    import numpy as np

    out = dict(_drawn_inputs(seed))
    spreads = {}
    factors = {'nsa_q_norm': 3.524,
     'nsa_k_norm': 4.257,
     'dil_q_norm': 3.908,
     'dil_k_norm': 4.141,
     'norm_post_ffn_2': 3.421,
     'pool_scale_2': 9.674,
     'gla_norm_2': 15.795,
     'mla_q_norm_2': 8.0,
     'mla_kv_norm_2': 8.0}
    for name, (base, spread) in spreads.items():
        noise = np.random.default_rng([zlib.crc32(name.encode()), seed]).standard_normal(out[name].shape)
        drawn = base * np.exp(spread * noise) if base else spread * noise
        out[name] = __import__('jax').numpy.asarray(drawn.astype(out[name].dtype))
    for name, factor in factors.items():
        out[name] = (out[name] * factor).astype(out[name].dtype)
    return out
```

```python
from contextlib import ExitStack, contextmanager

import numpy as np

import concourse.bass as bass
from concourse import mybir

F32 = mybir.dt.float32
F32R = mybir.dt.float32r
I32 = mybir.dt.int32
U32 = mybir.dt.uint32
ACT = mybir.ActivationFunctionType
ALU = mybir.AluOpType
AX_X = mybir.AxisListType.X

P = 128
SEQ = 512
TT = SEQ // P
D = 1024
DC = D // P
HD = 64
EPS = 1e-6
NEG = -1e30

NSA_PAIRS = 4
N_CMP = 31
CMP_BLOCK, CMP_STRIDE, CMP_HIDDEN = 32, 16, 256
KEYS, TOPK, HEADS = 128, 16, 8
Z_Q, Z_KC, Z_VC, Z_KS, Z_KW, Z_DIL, Z_MERGE, Z_CHUNKS = 0, 4, 5, 6, 7, 8, 20, 36

LAYERS = 2
Y_POOL, Y_GQ, Y_GK, Y_GR, Y_CQ, Y_CKV, Y_GATE, Y_MISC, Y_CHUNKS = 0, 4, 6, 8, 12, 15, 17, 41, 42
POOL_WINDOWS = (2, 4, 8, 16)
GLA_CHUNK = 64
D_FF = 2816
FC = D_FF // P
MLA_HEADS, MLA_QK, MLA_ROPE0 = 8, 96, 64

EG = 4
WT = 64
WTT = SEQ // WT
GROUPS = KEYS // EG
HALF_PI = float(np.pi / 2)
PI_DOWN = 3.1415925


def flat(ap):
    return ap.rearrange("p a b -> p (a b)")


class Stage:

    def __init__(self, nc, name):
        self.nc, self.name, self.sems, self.stack = nc, name, [], ExitStack()

    def __enter__(self):
        self.stack.__enter__()
        return self

    def sem(self, name):
        self.sems.append(self.nc.alloc_semaphore(f"{self.name}_{name}"))
        return self.sems[-1]

    def sb(self, name, shape, dt=F32):
        return self.stack.enter_context(self.nc.sbuf_tensor(f"{self.name}_{name}", shape, dt))

    def ps(self, name, shape):
        return self.stack.enter_context(self.nc.psum_tensor(f"{self.name}_{name}", shape, F32))

    def __exit__(self, *what):
        if what[0] is None:
            self.nc.clear_and_free_semaphores(self.sems)
            self.nc.all_engine_barrier()
        return self.stack.__exit__(*what)


class Memory:

    def __init__(self, nc):
        self.nc, self.stacks = nc, []

    @contextmanager
    def scope(self):
        with ExitStack() as stack:
            self.stacks.append(stack)
            yield
            self.stacks.pop()

    def sb(self, name, shape, dt=F32):
        return self.stacks[-1].enter_context(self.nc.sbuf_tensor(name, shape, dt))


class Steps:

    def __init__(self, eng, sem):
        self.eng, self.sem, self.base, self.n = eng, sem, 0, 0

    def at(self, base):
        self.base, self.n = base, 0

    def mark(self, ins):
        ins.then_inc(self.sem, 1)
        self.n += 1

    def wait(self):
        self.eng.wait_ge(self.sem, self.base + self.n)

    def after(self, ins):
        self.mark(ins)
        self.wait()


class Slot:

    def __init__(self, load, kc, x_hi, x_lo, width=P, tokens=None, keep=False):
        self.load, self.kc, self.x_hi, self.x_lo = load, kc, x_hi, x_lo
        self.width, self.tokens, self.keep = width, tokens, keep


def linear(nc, name, iters, slots, evac_on, evac, extra_sb=None, ahead=None):
    U = len(slots)
    lead = max(1, U // 2)
    with Stage(nc, name) as st:
        raw = [st.sb(f"raw{s}", [P, x.kc * x.width]) for s, x in enumerate(slots)]
        w_hi = [st.sb(f"w_hi{s}", [P, x.kc * x.width], F32R) for s, x in enumerate(slots)]
        w_lo = [st.sb(f"w_lo{s}", [P, x.kc * x.width], F32R) for s, x in enumerate(slots)]
        psum = [st.ps(f"ps{s}", [P, 512]) for s in range(U)]
        extra = extra_sb(st) if extra_sb else None
        raw_in = [st.sem(f"raw_in{s}") for s in range(U)]
        hi_done = st.sem("hi_done")
        lo_done = st.sem("lo_done")
        mm_done = st.sem("mm_done")
        bank_free = [st.sem(f"bank_free{s}") for s in range(U)]
        dve_steps = st.sem("dve_steps")

        def run(eng, body):
            if iters > 1:
                with eng.Fori(0, iters - 1) as i:
                    body(i, False)
            body(iters - 1, True)

        with nc.Block() as block:

            @block.sync
            def _(sp):
                def body(i, last):
                    for s, x in enumerate(slots):
                        sp.wait_ge(lo_done, i * U + (s + 1))
                        sp.dma_start(raw[s][:, :], x.load(i)).then_inc(raw_in[s], 16)

                run(sp, body)
                if ahead:
                    ahead.start(sp)

            @block.scalar
            def _(act):
                def high(i, s):
                    act.wait_ge(raw_in[s], i * 16 + 16)
                    act.wait_ge(mm_done, i * U + (s + 1))
                    nc.scalar.activation(w_hi[s][:, :], raw[s][:, :], ACT.Copy).then_inc(hi_done, 1)

                def body(i, last):
                    for s in range(U):
                        if not (last and s + lead >= U):
                            high(i + (s + lead) // U, (s + lead) % U)
                        if evac_on[s] == "act":
                            act.wait_ge(mm_done, i * U + (U + s + 1))
                            evac(act, i, s, psum[s], bank_free, extra)

                for s in range(lead):
                    high(0, s)
                for s in range(U):
                    if evac_on[s] == "act":
                        act.nop().then_inc(bank_free[s], 1)
                run(act, body)

            @block.vector
            def _(dve):
                steps = Steps(dve, dve_steps)

                def low(i, s):
                    dve.wait_ge(hi_done, i * U + (s + 1))
                    nc.vector.tensor_tensor(w_lo[s][:, :], raw[s][:, :], w_hi[s][:, :].bitcast(F32),
                                            ALU.subtract).then_inc(lo_done, 1)

                def body(i, last):
                    for s in range(U):
                        if not (last and s + lead >= U):
                            low(i + (s + lead) // U, (s + lead) % U)
                        if evac_on[s] == "dve":
                            dve.wait_ge(mm_done, i * U + (U + s + 1))
                            evac(dve, i, s, psum[s], bank_free, (extra, steps))

                dve.nop().then_inc(lo_done, U)
                for s in range(lead):
                    low(0, s)
                for s in range(U):
                    if evac_on[s] == "dve":
                        dve.nop().then_inc(bank_free[s], 1)
                run(dve, body)

            @block.tensor
            def _(pe):
                pe.nop().then_inc(mm_done, U)

                def body(i, last):
                    for s, x in enumerate(slots):
                        pe.wait_ge(lo_done, i * U + (U + s + 1))
                        pe.wait_ge(bank_free[s], i + 1)
                        for k in range(x.kc):
                            hi = w_hi[s][:, k * x.width:(k + 1) * x.width]
                            lo = w_lo[s][:, k * x.width:(k + 1) * x.width]
                            if x.tokens is None:
                                trio = [(hi, x.x_hi[:, k, :]), (hi, x.x_lo[:, k, :]), (lo, x.x_hi[:, k, :])]
                                out = psum[s][:, :]
                            else:
                                xh, xl = x.x_hi[:, k, x.tokens], x.x_lo[:, k, x.tokens]
                                trio = [(xh, hi), (xh, lo), (xl, hi)]
                                out = psum[s][:, 0:x.width]
                            for n, (a, b) in enumerate(trio):
                                mm = nc.tensor.matmul(out, a, b, start=(k == 0 and n == 0),
                                                      stop=(k == x.kc - 1 and n == 2))
                        mm.then_inc(mm_done, 1)

                run(pe, body)


def feature_major(nc, name, w, x_hi, x_lo, dst, unroll=4, ahead=None):
    n, kc = w.n, w.kc
    slots = [Slot(lambda i, s=s: w.chunk(i * unroll + s), kc, x_hi, x_lo) for s in range(unroll)]

    def evac(eng, i, s, ps, bank_free, extra):
        nc.scalar.activation(flat(dst[:, bass.ds(i * unroll + s, 1), :]), ps[:, :], ACT.Copy).then_inc(bank_free[s], 1)

    linear(nc, name, n // unroll, slots, ["act"] * unroll, evac, ahead=ahead)


class Weights:

    def __init__(self, ap, n, base=0):
        self.ap, self.n, self.base, self.kc = ap, n, base, ap.shape[2] // P

    def chunk(self, c):
        return chunk_of(self.ap, self.base + c)


def chunk_of(w, c):
    return w[bass.ds(c, 1)].rearrange("a p m -> p (a m)")


class Ahead:

    def __init__(self, st, name, pieces):
        self.pieces = pieces
        self.arrived = [st.sem(f"{name}_in{k}") for k in range(len(pieces))]

    def start(self, sp):
        for (dst, src), arrived in zip(self.pieces, self.arrived):
            sp.dma_start(dst, src).then_inc(arrived, 16)


def ahead_rows(st, name, w):
    raw = st.sb(f"{name}_raw", list(w.shape))
    return raw, Ahead(st, name, [(raw[:, k, :], w[:, k, :]) for k in range(w.shape[1])])


def token_major(nc, name, x_hi, x_lo, sets, raw=None, ahead=None):
    kc = x_hi.shape[1]
    wide = sets[0][0].shape[2]
    with Stage(nc, name) as st:
        if raw is None:
            raw = st.sb("raw", [P, kc, wide])
        raw_in = ahead.arrived if ahead else [st.sem(f"raw_in{k}") for k in range(kc)]
        w_hi = st.sb("w_hi", [P, kc, wide], F32R)
        w_lo = st.sb("w_lo", [P, kc, wide], F32R)
        psum = [st.ps(f"ps{s}", [P, 512]) for s in range(2)]
        hi_done, lo_done, mm_done, k_done, taken = (
            st.sem(x) for x in ("hi_done", "lo_done", "mm_done", "k_done", "taken"))
        with nc.Block() as block:

            @block.sync
            def _(sp):
                for i, (w, _, _) in enumerate(sets):
                    if i == 0 and ahead:
                        continue
                    for k in range(kc):
                        if i >= 1:
                            sp.wait_ge(lo_done, (i - 1) * kc + k + 1)
                        sp.dma_start(raw[:, k, 0:w.shape[2]], w[:, k, :]).then_inc(raw_in[k], 16)

            @block.scalar
            def _(act):
                def high(i, tiles_done=0):
                    width = sets[i][0].shape[2]
                    for k in range(kc):
                        act.wait_ge(raw_in[k], 16 * (i + 1))
                        if i >= 1 and k < kc - 1:
                            act.wait_ge(k_done, (i - 1) * (kc - 1) + k + 1)
                        elif i >= 1:
                            act.wait_ge(mm_done, tiles_done)
                        nc.scalar.activation(w_hi[:, k, 0:width], raw[:, k, 0:width], ACT.Copy).then_inc(hi_done, 1)

                high(0)
                n = 0
                for i, (w, tiles, dst) in enumerate(sets):
                    for j in range(len(tiles)):
                        if j == len(tiles) - 1 and i + 1 < len(sets):
                            high(i + 1, n + 1)
                        act.wait_ge(mm_done, n + 1)
                        nc.scalar.activation(dst[j], psum[n % 2][:, 0:w.shape[2]], ACT.Copy).then_inc(taken, 1)
                        n += 1

            @block.vector
            def _(dve):
                for i, (w, _, _) in enumerate(sets):
                    width = w.shape[2]
                    for k in range(kc):
                        dve.wait_ge(hi_done, i * kc + k + 1)
                        nc.vector.tensor_tensor(w_lo[:, k, 0:width], raw[:, k, 0:width],
                                                w_hi[:, k, 0:width].bitcast(F32), ALU.subtract).then_inc(lo_done, 1)

            @block.tensor
            def _(pe):
                n = 0
                for i, (w, tiles, _) in enumerate(sets):
                    width = w.shape[2]
                    for j, tokens in enumerate(tiles):
                        if n >= 2:
                            pe.wait_ge(taken, n - 1)
                        for k in range(kc):
                            if j == 0:
                                pe.wait_ge(lo_done, i * kc + k + 1)
                            xh, xl = x_hi[:, k, tokens], x_lo[:, k, tokens]
                            for m, (a, b) in enumerate(((xh, w_hi), (xh, w_lo), (xl, w_hi))):
                                mm = nc.tensor.matmul(psum[n % 2][:, 0:width], a, b[:, k, 0:width],
                                                      start=(k == 0 and m == 0), stop=(k == kc - 1 and m == 2))
                            if k == kc - 1:
                                mm.then_inc(mm_done, 1)
                            elif j == len(tiles) - 1 and i + 1 < len(sets):
                                mm.then_inc(k_done, 1)
                        n += 1


def load(nc, name, pairs):
    with Stage(nc, name) as st:
        arrived = st.sem("arrived")
        with nc.Block() as block:

            @block.sync
            def _(sp):
                for dst, src in pairs:
                    sp.dma_start(dst, src).then_inc(arrived, 16)
                sp.wait_ge(arrived, 16 * len(pairs))


def rms_norm(nc, name, C, x, gain, kc, hi=None, lo=None, add_to=None):
    with Stage(nc, name) as st:
        pairs, odd = kc // 2, kc % 2
        sq = [st.sb(f"sq{j}", [P, SEQ]) for j in range(pairs + odd)]
        sq_odd = [st.sb(f"sq_odd{j}", [P, SEQ]) for j in range(2)]
        root = st.sb("root", [P, SEQ])
        rstd = st.sb("rstd", [P, SEQ])
        PLACES = 4
        normed = [st.sb(f"normed{j}", [P, SEQ]) for j in range(PLACES)]
        total = st.ps("total", [P, SEQ])
        squared, odd_squared, paired, summed, rooted, rstd_done, norm_done, hi_done, used = (
            st.sem(x) for x in ("squared", "odd_squared", "paired", "summed", "rooted", "rstd_done", "norm_done",
                                "hi_done", "used"))
        with nc.Block() as block:

            @block.scalar
            def _(act):
                for j in range(pairs + odd):
                    nc.scalar.activation(sq[j][:, :], x[:, 2 * j, :], ACT.Square).then_inc(squared, 1)
                act.wait_ge(summed, pairs + odd)
                nc.scalar.activation(root[:, :], total[:, :], ACT.Sqrt, bias=C.eps[:, 0:1],
                                     scale=1.0 / (kc * P)).then_inc(rooted, 1)
                if hi is not None:
                    for k in range(kc):
                        act.wait_ge(norm_done, k + 1)
                        nc.scalar.activation(hi[:, k, :], normed[k % PLACES][:, :], ACT.Copy).then_inc(hi_done, 1)

            @block.tensor
            def _(pe):
                for j in range(pairs + odd):
                    if j < pairs:
                        pe.wait_ge(paired, j + 1)
                    else:
                        pe.wait_ge(squared, j + 1)
                    nc.tensor.matmul(total[:, :], C.ones[:, :], sq[j][:, :], start=(j == 0),
                                     stop=(j == pairs + odd - 1)).then_inc(summed, 1)

            @block.vector
            def _(dve):
                def square(j):
                    if j >= 2:
                        dve.wait_ge(paired, j - 1)
                    nc.vector.tensor_tensor(sq_odd[j % 2][:, :], x[:, 2 * j + 1, :], x[:, 2 * j + 1, :],
                                            ALU.mult).then_inc(odd_squared, 1)

                square(0)
                for j in range(pairs):
                    if j + 1 < pairs:
                        square(j + 1)
                    dve.wait_ge(odd_squared, j + 1)
                    dve.wait_ge(squared, j + 1)
                    nc.vector.tensor_tensor(sq[j][:, :], sq[j][:, :], sq_odd[j % 2][:, :], ALU.add).then_inc(paired, 1)

                def finish(j):
                    if hi is not None:
                        dve.wait_ge(hi_done, j + 1)
                        nc.vector.tensor_tensor(lo[:, j, :], normed[j % PLACES][:, :], hi[:, j, :].bitcast(F32),
                                                ALU.subtract).then_inc(used, 1)
                    else:
                        dve.wait_ge(norm_done, j + 1)
                        nc.vector.tensor_tensor(add_to[:, j, :], add_to[:, j, :], normed[j % PLACES][:, :],
                                                ALU.add).then_inc(used, 1)

                dve.wait_ge(rooted, 1)
                nc.vector.reciprocal(rstd[:, :], root[:, :]).then_inc(rstd_done, 1)
                dve.wait_ge(rstd_done, 1)
                lag = 2
                for k in range(kc + lag):
                    if k < kc:
                        if k >= PLACES:
                            dve.wait_ge(used, k - PLACES + 1)
                        nc.vector.scalar_tensor_tensor(out=normed[k % PLACES][:, :], in0=x[:, k, :],
                                                       scalar=gain[:, k:k + 1], in1=rstd[:, :],
                                                       op0=ALU.mult, op1=ALU.mult).then_inc(norm_done, 1)
                    if k >= lag:
                        finish(k - lag)


def split(nc, name, pairs):
    with Stage(nc, name) as st:
        hi_done = st.sem("hi_done")
        with nc.Block() as block:

            @block.scalar
            def _(act):
                for x, hi, _ in pairs:
                    nc.scalar.activation(hi, x, ACT.Copy).then_inc(hi_done, 1)

            @block.vector
            def _(dve):
                for n, (x, hi, lo) in enumerate(pairs):
                    dve.wait_ge(hi_done, n + 1)
                    nc.vector.tensor_tensor(lo, x, hi.bitcast(F32), ALU.subtract)


class Item:

    def __init__(self, src, dst, rows=slice(0, P), gain=None, group=None, dim=HD, cos=None, sin=None,
                 turn=None, times=None):
        self.src, self.dst, self.rows, self.gain, self.group, self.dim = src, dst, rows, gain, group, dim
        self.cos, self.sin, self.turn, self.times = cos, sin, turn, times


def norm_rope(nc, name, C, items):
    turning = items[0].turn is not None
    PLACES = 3
    with Stage(nc, name) as st:
        sq = [st.sb(f"sq{j}", [P, SEQ]) for j in range(2)]
        root = [st.sb(f"root{j}", [P, SEQ]) for j in range(2)]
        rstd = st.sb("rstd", [P, SEQ])
        normed = [st.sb(f"normed{j}", [P, SEQ]) for j in range(PLACES)]
        by_cos = [st.sb(f"by_cos{j}", [P, SEQ]) for j in range(2)]
        by_sin = [st.sb(f"by_sin{j}", [P, SEQ]) for j in range(PLACES)]
        sums = [st.ps(f"sums{j}", [P, SEQ]) for j in range(2)]
        turned = [st.ps(f"turned{j}", [P, SEQ]) for j in range(2)]
        squared, summed, rooted, rstd_done, norm_done, turn_done, cos_done, sin_done, item_done = (
            st.sem(x) for x in ("squared", "summed", "rooted", "rstd_done", "norm_done", "turn_done", "cos_done",
                                "sin_done", "item_done"))
        N = len(items)

        def width(it):
            return it.src.shape[1]

        with nc.Block() as block:

            @block.scalar
            def _(act):
                for n in range(N + 1):
                    if n < N:
                        it, w = items[n], width(items[n])
                        if n >= 2:
                            act.wait_ge(summed, n - 1)
                        nc.scalar.activation(sq[n % 2][it.rows, 0:w], it.src, ACT.Square).then_inc(squared, 1)
                    if n >= 1:
                        it, w, j = items[n - 1], width(items[n - 1]), (n - 1) % 2
                        act.wait_ge(summed, n)
                        if n >= 3:
                            act.wait_ge(norm_done, n - 2)
                        nc.scalar.activation(root[j][it.rows, 0:w], sums[j][it.rows, 0:w], ACT.Sqrt,
                                             bias=C.eps[it.rows, 0:1], scale=1.0 / it.dim).then_inc(rooted, 1)

            @block.tensor
            def _(pe):
                for n in range(N + 1):
                    if n < N:
                        it, w = items[n], width(items[n])
                        pe.wait_ge(squared, n + 1)
                        if n >= 2:
                            pe.wait_ge(rooted, n - 1)
                        nc.tensor.matmul(sums[n % 2][it.rows, 0:w], it.group, sq[n % 2][it.rows, 0:w],
                                         start=True, stop=True).then_inc(summed, 1)
                    if n >= 1 and turning:
                        m, it, w = n - 1, items[n - 1], width(items[n - 1])
                        pe.wait_ge(norm_done, m + 1)
                        if m >= 2:
                            pe.wait_ge(sin_done, m - 1)
                        nc.tensor.matmul(turned[m % 2][it.rows, 0:w], it.turn, normed[m % PLACES][it.rows, 0:w],
                                         start=True, stop=True).then_inc(turn_done, 1)

            @block.gpsimd
            def _(pool):
                def add(n):
                    it, w = items[n], width(items[n])
                    pool.wait_ge(cos_done, n + 1)
                    pool.wait_ge(sin_done, n + 1)
                    nc.gpsimd.tensor_tensor(it.dst, by_cos[n % 2][it.rows, 0:w], by_sin[n % PLACES][it.rows, 0:w],
                                            ALU.add).then_inc(item_done, 1)

                for n, it in enumerate(items):
                    w = width(it)
                    pool.wait_ge(norm_done, n + 1)
                    if turning:
                        if n >= 2:
                            pool.wait_ge(item_done, n - 1)
                        nc.gpsimd.tensor_tensor(by_cos[n % 2][it.rows, 0:w], normed[n % PLACES][it.rows, 0:w], it.cos,
                                                ALU.mult).then_inc(cos_done, 1)
                        if n >= 1:
                            add(n - 1)
                    else:
                        nc.gpsimd.tensor_tensor(it.dst, normed[n % PLACES][it.rows, 0:w], it.times,
                                                ALU.mult).then_inc(item_done, 1)
                if turning:
                    add(N - 1)

            @block.vector
            def _(dve):
                for n in range(N + 1):
                    if n < N:
                        it, w = items[n], width(items[n])
                        dve.wait_ge(rooted, n + 1)
                        if n >= 1:
                            dve.wait_ge(norm_done, n)
                        nc.vector.reciprocal(rstd[it.rows, 0:w], root[n % 2][it.rows, 0:w]).then_inc(rstd_done, 1)
                        dve.wait_ge(rstd_done, n + 1)
                        if n >= PLACES:
                            dve.wait_ge(item_done, n - PLACES + 1)
                        nc.vector.scalar_tensor_tensor(out=normed[n % PLACES][it.rows, 0:w], in0=it.src,
                                                       scalar=it.gain, in1=rstd[it.rows, 0:w],
                                                       op0=ALU.mult, op1=ALU.mult).then_inc(norm_done, 1)
                    if n >= 1 and turning:
                        m, it, w = n - 1, items[n - 1], width(items[n - 1])
                        dve.wait_ge(turn_done, m + 1)
                        if m >= PLACES:
                            dve.wait_ge(item_done, m - PLACES + 1)
                        nc.vector.tensor_tensor(by_sin[m % PLACES][it.rows, 0:w], turned[m % 2][it.rows, 0:w],
                                                it.sin, ALU.mult).then_inc(sin_done, 1)


class Unit:

    def __init__(self, scores, parts, values, rows, dst):
        self.scores, self.parts, self.values, self.rows, self.dst = scores, parts, values, rows, dst


def attention(nc, name, C, units, scale, cols, ahead=None):
    n_t = max(len(u.values) for u in units)
    n_p = max(len(u.parts) for u in units)
    score_banks, turned_banks = -(-cols // 512), -(-n_t // 4)
    places = 2 if 2 * score_banks + turned_banks + 2 <= 8 else 1
    with Stage(nc, name) as st:
        scores_at = [st.ps(f"scores{j}", [P, score_banks * 512]) for j in range(places)]
        turned = st.ps("turned", [P, turned_banks * 512])
        mixed = [st.ps(f"mixed{j}", [P, 512]) for j in range(2)]
        probs = [st.sb(f"probs{j}", [P, cols]) for j in range(2)]
        probs_t = [st.sb(f"probs_t{j}", [P, n_t * P]) for j in range(2)]
        top = [st.sb(f"top{j}", [P, n_p]) for j in range(2)]
        bias = [st.sb(f"bias{j}", [P, n_p]) for j in range(2)]
        den = [st.sb(f"den{j}", [P, n_p]) for j in range(2)]
        rden = [st.sb(f"rden{j}", [P, n_p]) for j in range(2)]
        wgt = [st.sb(f"wgt{j}", [P, n_p]) for j in range(2)]
        (zeroed, scored, max_done, exp_done, scaled, turn_done, copied_v, copied_s, mix_done, stored, dve_steps) = (
            st.sem(x) for x in ("zeroed", "scored", "max_done", "exp_done", "scaled", "turn_done", "copied_v",
                                "copied_s", "mix_done", "stored", "dve_steps"))
        N = len(units)
        with nc.Block() as block:

            @block.sync
            def _(sp):
                if ahead:
                    ahead.start(sp)

            @block.tensor
            def _(pe):
                def score(n):
                    scores = scores_at[n % places]
                    if n >= places:
                        pe.wait_ge(exp_done, n - places + 1)
                    for col, w, q, keys, mcol, mw, mask in units[n].scores:
                        if mcol > col:
                            nc.tensor.matmul(scores[:, col:mcol], q, keys[:, 0:mcol - col], start=True, stop=True)
                        out = scores[:, mcol:mcol + mw]
                        nc.tensor.matmul(out, q, keys[:, mcol - col:w], start=True, stop=False)
                        mm = nc.tensor.matmul(out, C.ident, mask, start=False, stop=True)
                    mm.then_inc(scored, 1)

                def wait_copied(n):
                    if n >= 1:
                        pe.wait_ge(copied_v, n)
                    by_scalar = sum(len(u.values) > 4 for u in units[:n])
                    if by_scalar:
                        pe.wait_ge(copied_s, by_scalar)

                for n in range(places):
                    score(n)
                for n in range(N + 1):
                    if n < N:
                        if n + places < N:
                            score(n + places)
                        pe.wait_ge(scaled, n + 1)
                        wait_copied(n)
                        for j, (col, _) in enumerate(units[n].values):
                            mm = nc.tensor.transpose(turned[:, j * P:(j + 1) * P], probs[n % 2][:, col:col + P],
                                                     C.ident[:, :])
                        mm.then_inc(turn_done, 1)
                    if n >= 1:
                        wait_copied(n)
                        if n >= 3:
                            pe.wait_ge(stored, n - 2)
                        values = units[n - 1].values
                        for j, (_, v) in enumerate(values):
                            mm = nc.tensor.matmul(mixed[(n - 1) % 2][:, 0:P], v,
                                                  probs_t[(n - 1) % 2][:, j * P:(j + 1) * P], start=(j == 0),
                                                  stop=(j == len(values) - 1))
                        mm.then_inc(mix_done, 1)

            @block.vector
            def _(dve):
                steps = Steps(dve, dve_steps)
                for j in range(2):
                    nc.vector.memset(probs[j][:, :], 0.0).then_inc(zeroed, 1)

                def largest(n):
                    u, scores = units[n], scores_at[n % places]
                    dve.wait_ge(scored, n + 1)
                    if n >= 2:
                        dve.wait_ge(exp_done, n - 1)
                    for j, (col, w, _, _) in enumerate(u.parts):
                        steps.mark(nc.vector.tensor_reduce(top[n % 2][:, j:j + 1], scores[:, col:col + w], AX_X,
                                                           ALU.max, negate=True))
                    steps.wait()
                    k = len(u.parts)
                    nc.vector.tensor_scalar(bias[n % 2][:, 0:k], top[n % 2][:, 0:k], scale, None,
                                            ALU.mult).then_inc(max_done, 1)

                def weigh(n):
                    u = units[n]
                    k = len(u.parts)
                    dve.wait_ge(exp_done, n + 1)
                    steps.after(nc.vector.reciprocal(rden[n % 2][:, 0:k], den[n % 2][:, 0:k]))
                    weights = rden
                    if u.parts[0][2] is not None:
                        steps.after(nc.vector.tensor_tensor(wgt[n % 2][:, 0:k], rden[n % 2][:, 0:k], u.parts[0][2],
                                                            ALU.mult))
                        weights = wgt
                    for j, (col, w, _, keep) in enumerate(u.parts):
                        pr, s = probs[n % 2][:, col:col + w], weights[n % 2][:, j:j + 1]
                        if keep is None:
                            ins = nc.vector.tensor_scalar(pr, pr, s, None, ALU.mult)
                        else:
                            ins = nc.vector.scalar_tensor_tensor(out=pr, in0=pr, scalar=s, in1=keep,
                                                                 op0=ALU.mult, op1=ALU.mult)
                    ins.then_inc(scaled, 1)

                def copy(n):
                    dve.wait_ge(turn_done, n + 1)
                    if n >= 2:
                        dve.wait_ge(mix_done, n - 1)
                    h = min(4, len(units[n].values))
                    nc.vector.tensor_copy(probs_t[n % 2][:, 0:h * P], turned[:, 0:h * P]).then_inc(copied_v, 1)

                for n in range(places):
                    largest(n)
                for n in range(N):
                    weigh(n)
                    if n + places < N:
                        largest(n + places)
                    copy(n)

            @block.scalar
            def _(act):
                act.wait_ge(zeroed, 2)

                def exps(n):
                    act.wait_ge(max_done, n + 1)
                    if n >= 2:
                        act.wait_ge(turn_done, n - 1)
                    scores = scores_at[n % places]
                    for j, (col, w, _, _) in enumerate(units[n].parts):
                        ins = nc.scalar.activation(probs[n % 2][:, col:col + w], scores[:, col:col + w], ACT.Exp,
                                                   bias=bias[n % 2][:, j:j + 1], scale=scale,
                                                   accum_out=den[n % 2][:, j:j + 1])
                    ins.then_inc(exp_done, 1)

                def store(n):
                    act.wait_ge(mix_done, n + 1)
                    u = units[n]
                    nc.scalar.activation(u.dst, mixed[n % 2][u.rows, 0:P], ACT.Copy).then_inc(stored, 1)

                exps(0)
                for n, u in enumerate(units):
                    if n + 1 < N:
                        exps(n + 1)
                    h, k = 4, len(u.values)
                    if k > h:
                        act.wait_ge(turn_done, n + 1)
                        if n >= 2:
                            act.wait_ge(mix_done, n - 1)
                        nc.scalar.activation(probs_t[n % 2][:, h * P:k * P], turned[:, h * P:k * P],
                                             ACT.Copy).then_inc(copied_s, 1)
                    if n >= 1:
                        store(n - 1)
                store(N - 1)


class Compressing:

    def __init__(self, st, name, z, pe, w1, w2, out, transposed):
        self.z, self.out, self.transposed = z, out, transposed
        self.w1 = st.sb(f"w1_{name}", [P, CMP_BLOCK, CMP_HIDDEN])
        self.w2 = st.sb(f"w2_{name}", [P, 2, P])
        self.pe = st.sb(f"pe_{name}", [P, CMP_BLOCK])
        self.loads = []
        for half in range(2):
            rows = slice(64 * half, 64 * half + 64)
            self.loads += [(self.pe[rows, :], pe), (self.w1[rows, :, :], w1.rearrange("(i d) h -> d i h", d=HD)),
                           (self.w2[:, :, rows], w2.rearrange("(a p) d -> p a d", p=P))]


def compress(nc, name, C, both, ahead, gates):
    per_group = SEQ // CMP_STRIDE
    blocks = 2 * per_group - 1
    with Stage(nc, name) as st:
        early, late = st.sb("early", [P, 2, SEQ]), st.sb("late", [P, 2, SEQ])
        by_block = st.sb("by_block", [blocks, CMP_HIDDEN])
        hidden = [st.sb(f"hidden{c}", [P, 2, blocks]) for c in range(2)]
        ps_h = [st.ps(f"ps_h{c}", [P, CMP_HIDDEN]) for c in range(2)]
        ps_t = st.ps("ps_t", [P, 2, blocks])
        ps_o = [st.ps(f"ps_o{c}", [P, 2 * P]) for c in range(2)]
        cleared, added, mm1, gelu_done, turn_done, hidden_done, mm2, out_cleared = (
            st.sem(x) for x in ("cleared", "added", "mm1", "gelu_done", "turn_done", "hidden_done", "mm2",
                                "out_cleared"))
        with nc.Block() as block:

            @block.vector
            def _(dve):
                nc.vector.memset(early[:, :, :], 0.0).then_inc(cleared, 1)
                nc.vector.memset(late[:, :, :], 0.0).then_inc(cleared, 1)
                for c, one in enumerate(both):
                    nc.vector.memset(one.out[:, :], 0.0).then_inc(out_cleared, 1)
                    dve.wait_ge(cleared, 2)
                    if c >= 1:
                        dve.wait_ge(mm1, c)
                    for n in (0, 3):
                        dve.wait_ge(ahead.arrived[6 * c + n], 16)
                    for g in range(2):
                        rows = slice(64 * g, 64 * g + 64)
                        for t, first in ((early, 0), (late, CMP_STRIDE)):
                            nc.vector.tensor_tensor(
                                t[rows, g, :].rearrange("p (c i) -> p c i", i=CMP_STRIDE),
                                one.z.rearrange("p (c i) -> p c i", i=CMP_STRIDE)[rows],
                                one.pe[rows, first:first + CMP_STRIDE].unsqueeze(1).to_broadcast(
                                    [64, SEQ // CMP_STRIDE, CMP_STRIDE]), ALU.add).then_inc(added, 1)
                for c, one in enumerate(both):
                    dve.wait_ge(mm2, c + 1)
                    dve.wait_ge(out_cleared, c + 1)
                    if one.transposed:
                        nc.vector.tensor_copy(one.out[0:64, :], ps_o[c][0:64, 0:N_CMP])
                        nc.vector.tensor_copy(one.out[64:P, :], ps_o[c][64:P, per_group:per_group + N_CMP])
                    else:
                        nc.vector.tensor_copy(one.out[0:N_CMP, :], ps_o[c][0:N_CMP, 0:P])

            @block.tensor
            def _(pe):
                span = CMP_STRIDE * (blocks - 1) + 1
                for c, one in enumerate(both):
                    for n in (1, 2, 4, 5):
                        pe.wait_ge(ahead.arrived[6 * c + n], 16)
                    pe.wait_ge(added, 4 * c + 4)
                    for i in range(CMP_BLOCK):
                        src = early if i < CMP_STRIDE else late
                        mm = nc.tensor.matmul(ps_h[c][0:blocks, :], flat(src[:, :, :])[:, i:i + span:CMP_STRIDE],
                                              one.w1[:, i, :], start=(i == 0), stop=(i == CMP_BLOCK - 1))
                    mm.then_inc(mm1, 1)
                for c, one in enumerate(both):
                    pe.wait_ge(gelu_done, c + 1)
                    if c >= 1:
                        pe.wait_ge(hidden_done, c)
                    for h in range(2):
                        mm = nc.tensor.transpose(ps_t[:, h, :], by_block[:, h * P:(h + 1) * P],
                                                 C.ident[0:blocks, 0:blocks])
                    mm.then_inc(turn_done, 1)
                    pe.wait_ge(hidden_done, c + 1)
                    if one.transposed:
                        for h in range(2):
                            mm = nc.tensor.matmul(ps_o[c][:, 0:blocks], one.w2[:, h, :], hidden[c][:, h, :],
                                                  start=(h == 0), stop=(h == 1))
                    else:
                        for g in range(2):
                            for h in range(2):
                                mm = nc.tensor.matmul(ps_o[c][0:N_CMP, g * 64:g * 64 + 64],
                                                      hidden[c][:, h, g * per_group:g * per_group + N_CMP],
                                                      one.w2[:, h, 0:64], start=(h == 0), stop=(h == 1))
                    mm.then_inc(mm2, 1)

            @block.scalar
            def _(act):
                for g in gates:
                    nc.scalar.activation(g, g, ACT.Sigmoid)
                for c in range(2):
                    act.wait_ge(mm1, c + 1)
                    if c >= 1:
                        act.wait_ge(turn_done, c)
                    nc.scalar.activation(by_block[:, :], ps_h[c][0:blocks, :],
                                         ACT.Gelu_apprx_tanh).then_inc(gelu_done, 1)
                    act.wait_ge(turn_done, c + 1)
                    nc.scalar.activation(hidden[c][:, :, :], ps_t[:, :, :], ACT.Copy).then_inc(hidden_done, 1)


def act_in_place(nc, name, func, aps):
    with Stage(nc, name):
        with nc.Block() as block:

            @block.scalar
            def _(act):
                for a in aps:
                    nc.scalar.activation(a, a, func)


def gated_merge(nc, name, weights, inputs, gates, hi=None, lo=None):
    J = len(weights)
    slots = [Slot(lambda i, j=j: weights[j].chunk(i), weights[j].kc, *inputs[j])
             for j in range(J)]
    per = J - 1 + (2 if hi is not None else 0)

    def extra(st):
        return st.sb("term", [P, SEQ]), st.sb("sum", [P, SEQ]) if hi is not None else None

    def evac(eng, i, s, ps, bank_free, more):
        (term, total), steps = more
        gate = flat(gates[:, bass.ds(i + DC * s, 1), :])
        if s == 0:
            steps.at(i * per)
        total = total[:, :] if hi is not None else flat(gates[:, bass.ds(i, 1), :])
        to = total if s == 0 else term[:, :]
        nc.vector.tensor_tensor(to, ps[:, :], gate, ALU.mult).then_inc(bank_free[s], 1)
        eng.wait_ge(bank_free[s], i + 2)
        if s:
            steps.after(nc.vector.tensor_tensor(total, total, term[:, :], ALU.add))
        if s == J - 1 and hi is not None:
            hi_n, lo_n = (flat(t[:, bass.ds(i, 1), :]) for t in (hi, lo))
            steps.after(nc.vector.tensor_copy(hi_n, total))
            steps.after(nc.vector.tensor_tensor(lo_n, total, hi_n.bitcast(F32), ALU.subtract))

    linear(nc, name, DC, slots, ["dve"] * J, evac, extra)


def expert_choice(nc, name, C, q, subkeys, chosen):
    H2 = 2 * HEADS
    with Stage(nc, name) as st:
        keys_sb = st.sb("keys", [P, KEYS])
        sc = st.sb("sc", [P, H2, KEYS])
        sc2 = st.sb("sc2", [P, H2, KEYS])
        best = st.sb("best", [P, H2, TOPK])
        at = st.sb("at", [P, H2, TOPK], U32)
        at_f = st.sb("at_f", [P, H2, TOPK])
        cand = st.sb("cand", [P, HEADS, TOPK * TOPK])
        cand2 = st.sb("cand2", [P, HEADS, TOPK * TOPK])
        top = st.sb("top", [P, HEADS, TOPK])
        ci = st.sb("ci", [P, HEADS, TOPK], U32)
        ij = st.sb("ij", [P, 2, HEADS, TOPK], U32)
        ij_f = st.sb("ij_f", [P, 2, HEADS, TOPK])
        eq = st.sb("eq", [P, HEADS, TOPK, TOPK])
        picked = st.sb("picked", [P, HEADS, TOPK, TOPK])
        total = st.sb("total", [P, HEADS])
        found = st.sb("found", [P, 3, P])
        ps = st.ps("ps", [P, H2, KEYS])
        ps_t = st.ps("ps_t", [P, 512])
        keys_in, scored, copied, sc_free, exp_ready, exp_done, found_done, turn_done, turn_free, dve_steps = (
            st.sem(x) for x in ("keys_in", "scored", "copied", "sc_free", "exp_ready", "exp_done",
                                "found_done", "turn_done", "turn_free", "dve_steps"))

        def found_of(j):
            return found[:, j, :].rearrange("p (h k) -> p h k", h=HEADS)

        with nc.Block() as block:

            @block.sync
            def _(sp):
                sp.dma_start(keys_sb[:, :], subkeys).then_inc(keys_in, 16)

            @block.tensor
            def _(pe):
                pe.wait_ge(keys_in, 16)
                for t in range(TT + 1):
                    if t < TT:
                        if t >= 1:
                            pe.wait_ge(copied, t)
                        for side in range(2):
                            rows = slice(64 * side, 64 * side + 64)
                            for h in range(HEADS):
                                mm = nc.tensor.matmul(ps[:, side * HEADS + h, :], q[rows, h, t * P:(t + 1) * P],
                                                      keys_sb[rows, :], start=True, stop=True)
                        mm.then_inc(scored, 1)
                    if t >= 1:
                        pe.wait_ge(found_done, t)
                        if t >= 2:
                            pe.wait_ge(turn_free, t - 1)
                        for j in range(3):
                            mm = nc.tensor.transpose(ps_t[:, j * P:(j + 1) * P], found[:, j, :], C.ident[:, :])
                        mm.then_inc(turn_done, 1)

            @block.scalar
            def _(act):
                with act.Fori(0, TT) as t:
                    act.wait_ge(scored, t + 1)
                    act.wait_ge(sc_free, t + 1)
                    for b in range(4):
                        ins = nc.scalar.activation(sc[:, 4 * b:4 * b + 4, :], ps[:, 4 * b:4 * b + 4, :], ACT.Copy)
                    ins.then_inc(copied, 1)
                    act.wait_ge(exp_ready, t + 1)
                    nc.scalar.activation(found[:, 2, :], found[:, 2, :], ACT.Exp).then_inc(exp_done, 1)

            @block.vector
            def _(dve):
                steps = Steps(dve, dve_steps)
                V = nc.vector
                dve.nop().then_inc(sc_free, 1)

                def sixteen(n, src, src2, out, index):
                    for j in range(n):
                        steps.mark(V.max(out[:, j, 0:8], src[:, j, :]))
                    steps.wait()
                    for j in range(n):
                        steps.mark(V.match_replace(src2[:, j, :], out[:, j, 0:8], src[:, j, :], -3e38))
                        steps.mark(V.max_index(index[:, j, 0:8], out[:, j, 0:8], src[:, j, :]))
                    steps.wait()
                    for j in range(n):
                        steps.mark(V.max(out[:, j, 8:16], src2[:, j, :]))
                    steps.wait()
                    for j in range(n):
                        steps.mark(V.max_index(index[:, j, 8:16], out[:, j, 8:16], src2[:, j, :]))
                    steps.wait()

                def tile(t):
                    dve.wait_ge(copied, t + 1)
                    sixteen(H2, sc, sc2, best, at)
                    V.tensor_copy(at_f[:, :, :], at[:, :, :]).then_inc(sc_free, 1)
                    dve.wait_ge(sc_free, t + 2)
                    wide = [P, HEADS, TOPK, TOPK]
                    steps.after(V.tensor_tensor(cand[:, :, :].rearrange("p h (i j) -> p h i j", i=TOPK),
                                                best[:, 0:HEADS, :].unsqueeze(3).to_broadcast(wide),
                                                best[:, HEADS:H2, :].unsqueeze(2).to_broadcast(wide), ALU.add))
                    sixteen(HEADS, cand, cand2, top, ci)
                    dve.wait_ge(turn_done, t + 1)
                    V.tensor_tensor(found_of(2), top[:, :, :], top[:, :, 0:1].to_broadcast([P, HEADS, TOPK]),
                                    ALU.subtract).then_inc(exp_ready, 1)
                    steps.mark(V.tensor_scalar(ij[:, 0, :, :], ci[:, :, :], 4, None, ALU.logical_shift_right))
                    steps.after(V.tensor_scalar(ij[:, 1, :, :], ci[:, :, :], 15, None, ALU.bitwise_and))
                    steps.after(V.tensor_copy(ij_f[:, :, :, :], ij[:, :, :, :]))
                    for side in range(2):
                        steps.after(V.tensor_tensor(
                            eq[:, :, :, :], C.iota[:, 0:TOPK].unsqueeze(1).unsqueeze(1).to_broadcast(wide),
                            ij_f[:, side, :, :].unsqueeze(3).to_broadcast(wide), ALU.is_equal))
                        steps.after(V.tensor_tensor(
                            picked[:, :, :, :], eq[:, :, :, :],
                            at_f[:, side * HEADS:(side + 1) * HEADS, :].unsqueeze(2).to_broadcast(wide), ALU.mult))
                        steps.after(V.tensor_reduce(found_of(side), picked[:, :, :, :], AX_X, ALU.add))
                    dve.wait_ge(exp_done, t + 1)
                    steps.after(V.tensor_reduce(total[:, :], found_of(2), AX_X, ALU.add))
                    steps.after(V.reciprocal(total[:, :], total[:, :]))
                    V.tensor_tensor(found_of(2), found_of(2), total[:, :].unsqueeze(2).to_broadcast([P, HEADS, TOPK]),
                                    ALU.mult).then_inc(found_done, 1)
                    dve.wait_ge(turn_done, t + 2)
                    V.tensor_copy(chosen[:, :, bass.ds(t * P, P)],
                                  ps_t[:, 0:3 * P].rearrange("p (j t) -> p j t", j=3)).then_inc(turn_free, 1)

                dve.nop().then_inc(turn_done, 1)
                for t in range(TT):
                    tile(t)


def expert_weights(nc, name, C, chosen, w_dram):
    QUAD, RING = 4, 4
    BUILT = 3
    per = WT // (QUAD * RING)
    with Stage(nc, name) as st:
        hot = [st.sb(f"hot{b}", [P, 2, QUAD, KEYS]) for b in range(RING)]
        built = [st.sb(f"built{b}", [P, KEYS, WT]) for b in range(BUILT)]
        ps = [st.ps(f"ps{b}", [P, QUAD, KEYS]) for b in range(RING)]
        hot_done, weighed, mm_done, taken = (st.sem(x) for x in ("hot_done", "weighed", "mm_done", "taken"))
        stored = [st.sem(f"stored{b}") for b in range(BUILT)]

        def quads(eng, body, before=None):
            for tt in range(WTT):
                if before:
                    before(tt)
                with eng.Fori(0, per) as j:
                    for b in range(RING):
                        body(tt, b, j * RING + (tt * per * RING + b), j * (RING * QUAD) + b * QUAD)

        with nc.Block() as block:

            @block.vector
            def _(dve):
                def body(tt, b, quad, tok):
                    dve.wait_ge(mm_done, quad + 1)
                    shape = [P, 2, QUAD, KEYS]
                    nc.vector.tensor_tensor(hot[b][:, :, :, :], C.iota[:, :].unsqueeze(1).unsqueeze(1).to_broadcast(shape),
                                            chosen[:, 0:2, bass.ds(tok + tt * WT, QUAD)].unsqueeze(3).to_broadcast(shape),
                                            ALU.is_equal).then_inc(hot_done, 1)

                quads(dve, body)

            @block.gpsimd
            def _(pool):
                def body(tt, b, quad, tok):
                    pool.wait_ge(hot_done, quad + 1)
                    nc.gpsimd.tensor_tensor(hot[b][:, 0, :, :], hot[b][:, 0, :, :],
                                            chosen[:, 2, bass.ds(tok + tt * WT, QUAD)].unsqueeze(2).to_broadcast(
                                                [P, QUAD, KEYS]), ALU.mult).then_inc(weighed, 1)

                quads(pool, body)

            @block.tensor
            def _(pe):
                def body(tt, b, quad, tok):
                    pe.wait_ge(weighed, quad + 1)
                    pe.wait_ge(taken, quad + 1)
                    for k in range(QUAD):
                        mm = nc.tensor.matmul(ps[b][:, k, :], hot[b][:, 0, k, :], hot[b][:, 1, k, :],
                                              start=True, stop=True)
                    mm.then_inc(mm_done, 1)

                pe.nop().then_inc(mm_done, RING)
                quads(pe, body)

            @block.scalar
            def _(act):
                def before(tt):
                    if tt >= BUILT:
                        act.wait_ge(stored[tt % BUILT], 16 * (tt // BUILT))

                def body(tt, b, quad, tok):
                    act.wait_ge(mm_done, quad + (RING + 1))
                    nc.scalar.activation(built[tt % BUILT][:, :, bass.ds(tok, QUAD)].rearrange("p e t -> p t e"),
                                         ps[b][:, :, :], ACT.Copy).then_inc(taken, 1)

                act.nop().then_inc(taken, RING)
                quads(act, body, before)

            @block.sync
            def _(sp):
                for tt in range(WTT):
                    sp.wait_ge(taken, RING + (tt + 1) * (WT // QUAD))
                    sp.dma_start(w_dram[tt], flat(built[tt % BUILT][:, :, :])).then_inc(stored[tt % BUILT], 16)
                for b in range(BUILT):
                    sp.wait_ge(stored[b], 16 * ((WTT - b + BUILT - 1) // BUILT))


def experts(nc, name, C, x, h_hi, h_lo, u, v, w_dram):
    with Stage(nc, name) as st:
        u_raw = [st.sb(f"u_raw{s}", [P, D]) for s in range(4)]
        u_hi = [st.sb(f"u_hi{s}", [P, D], F32R) for s in range(2)]
        u_lo = [st.sb(f"u_lo{s}", [P, D], F32R) for s in range(2)]
        v_raw = [st.sb(f"v_raw{s}", [P, D]) for s in range(2)]
        v_hi = st.sb("v_hi", [P, EG, D], F32R)
        v_lo = st.sb("v_lo", [P, EG, D], F32R)
        wgt = [st.sb(f"wgt{s}", [P, WTT, EG * WT]) for s in range(2)]
        gelu = [st.sb(f"gelu{s}", [P, SEQ]) for s in range(2)]
        prod = [st.sb(f"prod{s}", [P, SEQ]) for s in range(2)]
        a_hi = [st.sb(f"a_hi{s}", [P, EG, SEQ], F32R) for s in range(2)]
        a_lo = [st.sb(f"a_lo{s}", [P, EG, SEQ], F32R) for s in range(2)]
        ps_a = [st.ps(f"ps_a{s}", [P, SEQ]) for s in range(2)]
        ps_b = [st.ps(f"ps_b{s}", [P, SEQ]) for s in range(4)]
        u_in = [st.sem(f"u_in{s}") for s in range(4)]
        v_in = [st.sem(f"v_in{s}") for s in range(2)]
        w_in = [st.sem(f"w_in{s}") for s in range(2)]
        u_hi_done = st.sem("u_hi_done")
        u_lo_done = st.sem("u_lo_done")
        a_done = st.sem("a_done")
        gelu_done = st.sem("gelu_done")
        mult_done = st.sem("mult_done")
        a_hi_done = st.sem("a_hi_done")
        a_lo_done = st.sem("a_lo_done")
        v_hi_done = st.sem("v_hi_done")
        v_lo_done = st.sem("v_lo_done")
        b_done = st.sem("b_done")
        added = st.sem("added")

        v_rows = v.rearrange("(a b) d -> b a d", b=KEYS)

        def steps_of(eng, step):
            step(0, 0, True, False)
            with eng.Fori(0, GROUPS // 2 - 1) as i:
                step(i * 2 + 1, 1, False, False)
                step(i * 2 + 2, 0, False, False)
            step(GROUPS - 1, 1, False, False)
            step(GROUPS, 0, False, True)

        with nc.Block() as block:

            @block.sync
            def _(sp):
                def load_u(g, e):
                    sp.wait_ge(u_lo_done, g * EG + (e + 1))
                    sp.dma_start(u_raw[e][:, :], chunk_of(u, g * EG + e)).then_inc(u_in[e], 16)

                def load_v(g, e):
                    sp.wait_ge(v_lo_done, g * EG + (e + 1))
                    sp.dma_start(v_raw[e % 2][:, :], chunk_of(v_rows, g * EG + e)).then_inc(v_in[e % 2], 16)

                def load_w(g, par):
                    sp.dma_start(wgt[par][:, :, :],
                                 w_dram[:, :, bass.ds(g * (EG * WT), EG * WT)].rearrange("t p m -> p t m")
                                 ).then_inc(w_in[par], 16)

                for e in range(EG):
                    load_u(0, e)
                load_w(0, 0)
                load_w(1, 1)

                def step(g, par, first, last):
                    if last:
                        return
                    if not (isinstance(g, int) and g == GROUPS - 1):
                        if not first:
                            sp.wait_ge(mult_done, g * EG + 2)
                            load_w(g + 1, 1 - par)
                        for e in range(EG):
                            load_u(g + 1, e)
                    for e in range(EG):
                        load_v(g, e)

                steps_of(sp, step)

            @block.scalar
            def _(act):
                def high_u(g, e):
                    act.wait_ge(u_in[e], g * 16 + 16)
                    act.wait_ge(a_done, g * EG + (e + 1))
                    nc.scalar.activation(u_hi[e % 2][:, :], u_raw[e][:, :], ACT.Copy).then_inc(u_hi_done, 1)

                act.nop().then_inc(gelu_done, 2)
                high_u(0, 0)
                high_u(0, 1)

                def step(g, par, first, last):
                    for e in range(EG):
                        if not first:
                            act.wait_ge(v_in[e % 2], g * 32 + (16 * (e // 2) + 16 - 32))
                            act.wait_ge(b_done, g * DC + DC)
                            nc.scalar.activation(v_hi[:, e, :], v_raw[e % 2][:, :], ACT.Copy).then_inc(v_hi_done, 1)
                        if last:
                            continue
                        act.wait_ge(a_done, g * EG + (e + 3))
                        act.wait_ge(mult_done, g * EG + (e + 1))
                        nc.scalar.activation(gelu[e % 2][:, :], ps_a[e % 2][:, :],
                                             ACT.Gelu_apprx_tanh).then_inc(gelu_done, 1)
                        if e + 2 < EG:
                            high_u(g, e + 2)
                        elif not (isinstance(g, int) and g == GROUPS - 1):
                            high_u(g + 1, e + 2 - EG)
                        act.wait_ge(mult_done, g * EG + (e + 3))
                        act.wait_ge(b_done, g * DC + DC)
                        nc.scalar.activation(a_hi[par][:, e, :], prod[e % 2][:, :], ACT.Copy).then_inc(a_hi_done, 1)

                steps_of(act, step)

            @block.vector
            def _(dve):
                def low_u(g, e):
                    dve.wait_ge(u_hi_done, g * EG + (e + 1))
                    nc.vector.tensor_tensor(u_lo[e % 2][:, :], u_raw[e][:, :], u_hi[e % 2][:, :].bitcast(F32),
                                            ALU.subtract).then_inc(u_lo_done, 1)

                dve.nop().then_inc(u_lo_done, 4)
                dve.nop().then_inc(v_lo_done, 2)
                dve.nop().then_inc(mult_done, 2)
                dve.nop().then_inc(a_lo_done, 2)
                dve.nop().then_inc(added, DC)
                low_u(0, 0)
                low_u(0, 1)

                def step(g, par, first, last):
                    for e in range(EG):
                        if not first:
                            dve.wait_ge(v_hi_done, g * EG + (e + 1 - EG))
                            nc.vector.tensor_tensor(v_lo[:, e, :], v_raw[e % 2][:, :], v_hi[:, e, :].bitcast(F32),
                                                    ALU.subtract).then_inc(v_lo_done, 1)
                        if last:
                            continue
                        if e == 0:
                            dve.wait_ge(w_in[par], g * 8 + (16 - 8 * par))
                        dve.wait_ge(gelu_done, g * EG + (e + 3))
                        dve.wait_ge(a_lo_done, g * EG + (e + 1))
                        nc.vector.tensor_tensor(prod[e % 2][:, :].rearrange("p (a t) -> p a t", a=WTT),
                                                gelu[e % 2][:, :].rearrange("p (a t) -> p a t", a=WTT),
                                                wgt[par][:, :, e * WT:(e + 1) * WT], ALU.mult).then_inc(mult_done, 1)
                        if e + 2 < EG:
                            low_u(g, e + 2)
                        elif not (isinstance(g, int) and g == GROUPS - 1):
                            low_u(g + 1, e + 2 - EG)
                        dve.wait_ge(a_hi_done, g * EG + (e + 1))
                        nc.vector.tensor_tensor(a_lo[par][:, e, :], prod[e % 2][:, :],
                                                a_hi[par][:, e, :].bitcast(F32), ALU.subtract).then_inc(a_lo_done, 1)
                    if not first:
                        for d in range(DC):
                            dve.wait_ge(b_done, g * DC + (DC + d + 1))
                            dve.wait_ge(added, g * DC + (d + 1 - DC))
                            nc.vector.tensor_tensor(x[:, d, :], x[:, d, :], ps_b[d % 4][:, :],
                                                    ALU.add).then_inc(added, 1)

                steps_of(dve, step)

            @block.tensor
            def _(pe):
                pe.nop().then_inc(a_done, 2)
                pe.nop().then_inc(b_done, 2 * DC)

                def step(g, par, first, last):
                    if not last:
                        for e in range(EG):
                            pe.wait_ge(u_lo_done, g * EG + (e + 5))
                            pe.wait_ge(gelu_done, g * EG + (e + 1))
                            for k in range(DC):
                                hi, lo = (w[e % 2][:, k * P:(k + 1) * P] for w in (u_hi, u_lo))
                                for n, (a, b) in enumerate(((hi, h_hi), (hi, h_lo), (lo, h_hi))):
                                    mm = nc.tensor.matmul(ps_a[e % 2][:, :], a, b[:, k, :],
                                                          start=(k == 0 and n == 0), stop=(k == DC - 1 and n == 2))
                            mm.then_inc(a_done, 1)
                    if not first:
                        pe.wait_ge(v_lo_done, g * EG + 2)
                        pe.wait_ge(a_lo_done, g * EG + 2)
                        for d in range(DC):
                            pe.wait_ge(added, g * DC + (d + 1 - 4))
                            cols = slice(d * P, (d + 1) * P)
                            for e in range(EG):
                                hi, lo = v_hi[:, e, cols], v_lo[:, e, cols]
                                for n, (a, b) in enumerate(((hi, a_hi), (hi, a_lo), (lo, a_hi))):
                                    mm = nc.tensor.matmul(ps_b[d % 4][:, :], a, b[1 - par][:, e, :],
                                                          start=(e == 0 and n == 0), stop=(e == EG - 1 and n == 2))
                            mm.then_inc(b_done, 1)

                steps_of(pe, step)


def add_product(nc, name, w, x_hi, x_lo, x, unroll):
    n, kc = w.n, w.kc
    slots = [Slot(lambda i, s=s: w.chunk(i * unroll + s), kc, x_hi, x_lo) for s in range(unroll)]

    def evac(eng, i, s, ps, bank_free, more):
        o = flat(x[:, bass.ds(i * unroll + s, 1), :])
        nc.vector.tensor_tensor(o, o, ps[:, :], ALU.add).then_inc(bank_free[s], 1)

    linear(nc, name, n // unroll, slots, ["dve"] * unroll, evac)


def angles(nc, name, C, positions):
    rows = slice(MLA_ROPE0, MLA_QK)
    n = MLA_QK - MLA_ROPE0
    two_pi = 2 * np.pi
    c1 = 6.28125
    c2 = float(np.float32(np.floor((two_pi - c1) * 2 ** 21) / 2 ** 21))
    c3 = float(two_pi - c1 - c2)
    magic = 12582912.0
    with Stage(nc, name) as st:
        pos_i = st.sb("pos_i", [P, SEQ], I32)
        angle = st.sb("angle", [P, SEQ])
        turns = st.sb("turns", [P, SEQ])
        left = [st.sb(f"left{j}", [P, SEQ]) for j in range(2)]
        pos_in, reduced, dve_steps = (st.sem(x) for x in ("pos_in", "reduced", "dve_steps"))
        with nc.Block() as block:

            @block.sync
            def _(sp):
                sp.dma_start(pos_i[rows, :], positions.partition_broadcast(n)).then_inc(pos_in, 16)

            @block.vector
            def _(dve):
                steps = Steps(dve, dve_steps)
                V = nc.vector
                steps.mark(V.memset(C.cos2[:, :], 1.0))
                steps.mark(V.memset(C.sin2[:, :], 0.0))
                dve.wait_ge(pos_in, 16)
                steps.after(V.tensor_copy(angle[rows, :], pos_i[rows, :]))
                steps.after(V.tensor_scalar(angle[rows, :], angle[rows, :], C.inv_freq[rows, 0:1], None, ALU.mult))
                for j, (ahead, quarter) in enumerate(((0.0, 0.0), (0.25, HALF_PI))):
                    steps.after(V.tensor_scalar(turns[rows, :], angle[rows, :], float(1 / two_pi), ahead,
                                                ALU.mult, ALU.add))
                    steps.after(V.tensor_scalar(turns[rows, :], turns[rows, :], magic, None, ALU.add))
                    steps.after(V.tensor_scalar(turns[rows, :], turns[rows, :], -magic, None, ALU.add))
                    steps.after(V.scalar_tensor_tensor(out=left[j][rows, :], in0=turns[rows, :], scalar=-c1,
                                                       in1=angle[rows, :], op0=ALU.mult, op1=ALU.add))
                    for c in (c2, c3):
                        steps.after(V.scalar_tensor_tensor(out=left[j][rows, :], in0=turns[rows, :], scalar=-c,
                                                           in1=left[j][rows, :], op0=ALU.mult, op1=ALU.add))
                    steps.after(V.tensor_scalar(left[j][rows, :], left[j][rows, :], quarter, PI_DOWN,
                                                ALU.add, ALU.min))
                    V.tensor_scalar(left[j][rows, :], left[j][rows, :], -PI_DOWN, None,
                                    ALU.max).then_inc(reduced, 1)

            @block.scalar
            def _(act):
                for j, t in enumerate((C.sin2, C.cos2)):
                    act.wait_ge(reduced, j + 1)
                    nc.scalar.activation(t[rows, :], left[j][rows, :], ACT.Sin)


def pool_mixer(nc, name, C, u, w_pool, scale, gates):
    G = len(POOL_WINDOWS)
    with Stage(nc, name) as st:
        w_sb = st.sb("w", [P, G, P])
        sums = [st.sb(f"sums{j}", [P, SEQ]) for j in range(2)]
        diff = st.sb("diff", [P, G, SEQ])
        ps = [st.ps(f"ps{j}", [P, SEQ]) for j in range(G)]
        w_in, diff_done, mm_done, dve_steps = (st.sem(x) for x in ("w_in", "diff_done", "mm_done", "dve_steps"))
        with nc.Block() as block:

            @block.sync
            def _(sp):
                sp.dma_start(w_sb[:, :, :], w_pool).then_inc(w_in, 16)

            @block.scalar
            def _(act):
                nc.scalar.activation(gates, gates, ACT.Sigmoid)

            @block.vector
            def _(dve):
                steps = Steps(dve, dve_steps)
                V = nc.vector
                for g, window in enumerate(POOL_WINDOWS):
                    src, w, j = u[:, g, :], 1, 0
                    while w < window:
                        dst = sums[j]
                        steps.mark(V.tensor_copy(dst[:, 0:w], src[:, 0:w]))
                        steps.after(V.tensor_tensor(dst[:, w:SEQ], src[:, w:SEQ], src[:, 0:SEQ - w], ALU.add))
                        src, w, j = dst, 2 * w, 1 - j
                    steps.after(V.tensor_tensor(sums[j][:, :], src[:, 0:SEQ], C.inv_count[:, g, :], ALU.mult))
                    steps.after(V.tensor_tensor(diff[:, g, :], sums[j][:, :], u[:, g, :], ALU.subtract))
                    dve.nop().then_inc(diff_done, 1)
                for g in range(G):
                    dve.wait_ge(mm_done, g + 1)
                    V.tensor_scalar(u[:, g, :], ps[g][:, :], scale[:, g:g + 1], None, ALU.mult)

            @block.tensor
            def _(pe):
                pe.wait_ge(w_in, 16)
                for g in range(G):
                    pe.wait_ge(diff_done, g + 1)
                    nc.tensor.matmul(ps[g][:, :], w_sb[:, g, :], diff[:, g, :], start=True,
                                     stop=True).then_inc(mm_done, 1)


def gla_attention(nc, name, C, y, values, w_a2, mixed):
    q, k, low = y[:, Y_GQ:Y_GQ + 2, :], y[:, Y_GK:Y_GK + 2, :], y[0:16, Y_MISC, :]
    NCH = SEQ // GLA_CHUNK
    with Stage(nc, name) as st:
        low_1 = st.sb("low_1", [17, SEQ])
        w_sb = st.sb("w", [17, 256])
        size = st.sb("size", [P, TT * 256])
        log_a = st.sb("log_a", [P, TT, 256])
        up = st.sb("up", [P, 2, SEQ])
        down = st.sb("down", [P, 2, SEQ])
        to_end = st.sb("to_end", [P, TT, 256])
        q_dec = st.sb("q_dec", [P, 2, SEQ])
        k_inv = st.sb("k_inv", [P, 2, SEQ])
        k_end = st.sb("k_end", [P, TT, 256])
        att = st.sb("att", [P, TT, 4, P])
        state = st.sb("state", [P, 2, NCH, P])
        ps_g = st.ps("ps_g", [P, TT * 256])
        ps_c = [st.ps(f"ps_c{j}", [P, 512]) for j in range(2)]
        ps_k = [st.ps(f"ps_k{j}", [P, 512]) for j in range(2)]
        ps_o = [st.ps(f"ps_o{j}", [P, 512]) for j in range(2)]
        (w_in, ones_done, low_done, gates_mm, size_done, log_done, cum_mm, exp_done, dec_done, turn_mm, end_done,
         att_mm, att_done, kv_mm, state_done, out_mm, out_taken, act_steps, dve_steps) = (
            st.sem(x) for x in ("w_in", "ones_done", "low_done", "gates_mm", "size_done", "log_done", "cum_mm",
                                "exp_done", "dec_done", "turn_mm", "end_done", "att_mm", "att_done",
                                "kv_mm", "state_done", "out_mm", "out_taken", "act_steps", "dve_steps"))
        V, S = nc.vector, nc.scalar
        with nc.Block() as block:

            @block.sync
            def _(sp):
                sp.dma_start(w_sb[:, :], w_a2).then_inc(w_in, 16)

            @block.tensor
            def _(pe):
                mmul = nc.tensor.matmul
                pe.wait_ge(w_in, 16)
                pe.wait_ge(low_done, 1)
                for t in range(TT):
                    mm = mmul(ps_g[:, t * 256:(t + 1) * 256], low_1[:, t * P:(t + 1) * P], w_sb[:, :], start=True, stop=True)
                mm.then_inc(gates_mm, 1)
                pe.wait_ge(log_done, 1)
                for c in range(2):
                    for t in range(TT):
                        mm = mmul(ps_c[c][:, t * P:(t + 1) * P], log_a[:, t, c * P:(c + 1) * P], C.cum[:, :], start=True, stop=True)
                    mm.then_inc(cum_mm, 1)
                for t in range(TT):
                    if t >= 2:
                        pe.wait_ge(end_done, t - 1)
                    mmul(ps_k[t % 2][:, 0:256], C.rev[:, :], log_a[:, t, :], start=True, stop=True)
                    for c in range(2):
                        mm = nc.tensor.transpose(ps_k[t % 2][:, 256 + c * P:256 + (c + 1) * P], k[:, c, t * P:(t + 1) * P], C.ident[:, :])
                    mm.then_inc(turn_mm, 1)
                pe.wait_ge(dec_done, 4)
                for t in range(TT):
                    if t == 0:
                        pe.wait_ge(exp_done, 4)
                    else:
                        pe.wait_ge(att_done, 2 * t)
                    for h in range(4):
                        rows, cols = slice(64 * (h % 2), 64 * (h % 2) + 64), slice(t * P, (t + 1) * P)
                        col = 256 * (t % 2) + P * (h // 2)
                        mm = mmul(ps_c[h % 2][:, col:col + P], k_inv[rows, h // 2, cols], q_dec[rows, h // 2, cols], start=True, stop=True)
                    mm.then_inc(att_mm, 1)
                pe.wait_ge(end_done, TT)
                for n in range(NCH - 1):
                    if n >= 2:
                        pe.wait_ge(state_done, n - 1)
                    rows, t = slice(64 * (n % 2), 64 * (n % 2) + 64), n // 2
                    for pr in range(2):
                        mm = mmul(ps_k[n % 2][:, pr * 256:(pr + 1) * 256], k_end[rows, t, pr * P:(pr + 1) * P],
                                  values[rows, t, pr * 256:(pr + 1) * 256], start=True, stop=True)
                    mm.then_inc(kv_mm, 1)
                pe.wait_ge(att_done, 2 * TT)
                pe.wait_ge(state_done, NCH - 1)
                for h in range(4):
                    if h >= 2:
                        pe.wait_ge(out_taken, h - 1)
                    rows = slice(64 * (h % 2), 64 * (h % 2) + 64)
                    for n in range(NCH):
                        t, half = n // 2, slice(64 * (n % 2), 64 * (n % 2) + 64)
                        cols = slice(n * GLA_CHUNK, (n + 1) * GLA_CHUNK)
                        mm = mmul(ps_o[h % 2][:, cols], values[:, t, h * P:(h + 1) * P], att[:, t, h, half], start=True,
                                  stop=(n == 0))
                        if n:
                            mm = mmul(ps_o[h % 2][:, cols], state[rows, h // 2, n, :], q_dec[rows, h // 2, cols],
                                      start=False, stop=True)
                    mm.then_inc(out_mm, 1)

            @block.scalar
            def _(act):
                act.wait_ge(ones_done, 1)
                S.activation(low_1[0:16, :], low, ACT.Copy).then_inc(low_done, 1)
                steps = Steps(act, act_steps)
                act.wait_ge(gates_mm, 1)
                for f, kw in ((ACT.Abs, {}), (ACT.Exp, {"scale": -1.0}), (ACT.Ln, {"bias": C.ones[:, 0:1]})):
                    for b in range(2):
                        half = slice(512 * b, 512 * b + 512)
                        steps.mark(S.activation(size[:, half], ps_g[:, half] if f == ACT.Abs else size[:, half], f, **kw))
                    steps.wait()
                act.nop().then_inc(size_done, 1)
                for c in range(2):
                    act.wait_ge(cum_mm, c + 1)
                    S.activation(up[:, c, :], ps_c[c][:, :], ACT.Exp).then_inc(exp_done, 1)
                    S.activation(down[:, c, :], ps_c[c][:, :], ACT.Exp, scale=-1.0).then_inc(exp_done, 1)
                for t in range(TT):
                    act.wait_ge(turn_mm, t + 1)
                    S.activation(to_end[:, t, :], ps_k[t % 2][:, 0:256], ACT.Exp).then_inc(exp_done, 1)
                for h in range(4):
                    act.wait_ge(out_mm, h + 1)
                    S.activation(mixed[:, h, :], ps_o[h % 2][:, :], ACT.Copy).then_inc(out_taken, 1)

            @block.vector
            def _(dve):
                steps = Steps(dve, dve_steps)
                V.memset(low_1[:, :], 1.0).then_inc(ones_done, 1)
                steps.mark(V.memset(state[:, :, 0, :], 0.0))
                dve.wait_ge(size_done, 1)
                for b in range(2):
                    ins = V.scalar_tensor_tensor(out=flat(log_a[:, 2 * b:2 * b + 2, :]), in0=ps_g[:, 512 * b:512 * b + 512],
                                                 scalar=0.0, in1=size[:, 512 * b:512 * b + 512], op0=ALU.min, op1=ALU.subtract)
                ins.then_inc(log_done, 1)
                for c in range(2):
                    dve.wait_ge(exp_done, 2 * c + 2)
                    V.scalar_tensor_tensor(out=q_dec[:, c, :], in0=q[:, c, :], scalar=HD ** -0.5, in1=up[:, c, :],
                                           op0=ALU.mult, op1=ALU.mult).then_inc(dec_done, 1)
                    V.tensor_tensor(k_inv[:, c, :], k[:, c, :], down[:, c, :], ALU.mult).then_inc(dec_done, 1)
                for t in range(TT):
                    dve.wait_ge(turn_mm, t + 1)
                    dve.wait_ge(exp_done, 4 + t + 1)
                    V.tensor_tensor(k_end[:, t, :], to_end[:, t, :], ps_k[t % 2][:, 256:512], ALU.mult).then_inc(end_done, 1)
                for t in range(TT):
                    dve.wait_ge(att_mm, t + 1)
                    for odd in range(2):
                        got = ps_c[odd][:, 256 * (t % 2):256 * (t % 2) + 256]
                        V.tensor_tensor(att[:, t, odd:4:2, :], got.rearrange("p (h t) -> p h t", h=2),
                                        C.same[:, :].unsqueeze(1).to_broadcast([P, 2, P]), ALU.mult).then_inc(att_done, 1)
                for n in range(NCH - 1):
                    dve.wait_ge(kv_mm, n + 1)
                    steps.wait()
                    last = GLA_CHUNK * (n + 1) - 1
                    for pr in range(2):
                        for h in range(2):
                            rows = slice(64 * h, 64 * h + 64)
                            ins = V.scalar_tensor_tensor(
                                out=state[rows, pr, n + 1, :], in0=state[rows, pr, n, :], scalar=up[rows, pr, last:last + 1],
                                in1=ps_k[n % 2][rows, pr * 256 + h * P:pr * 256 + (h + 1) * P], op0=ALU.mult, op1=ALU.add)
                            if pr == 1 and h == 1:
                                ins.then_inc(state_done, 1)
                    dve.wait_ge(state_done, n + 1)


def gla_mixer(nc, name, C, y, values, w_a2, g_norm):
    r = y[:, Y_GR:Y_GR + 4, :]
    with nc.sbuf_tensor(name + "_mixed", [P, 4, SEQ], F32) as mixed:
        gla_attention(nc, name, C, y, values, w_a2, mixed)
        act_in_place(nc, name + "_silu", ACT.Silu, [flat(r)])
        norm_rope(nc, name + "_norm", C, [Item(mixed[:, h, :], r[:, h, :], gain=g_norm[:, h:h + 1], group=C.ones,
                                               dim=P, times=r[:, h, :]) for h in range(4)])


def gated_ffn(nc, name, w_gu, x_hi, x_lo, a_hi, a_lo):
    slots = [Slot(lambda i, s=s: w_gu.chunk(i * 4 + s), DC, x_hi, x_lo) for s in range(4)]

    def extra(st):
        return [st.sb(f"silu{j}", [P, SEQ]) for j in range(2)], st.sb("both", [P, SEQ])

    def evac(eng, i, s, ps, bank_free, more):
        if s % 2 == 0:
            silu, _ = more
            eng.wait_ge(bank_free[s + 1], i + 1)
            nc.scalar.activation(silu[s // 2][:, :], ps[:, :], ACT.Silu).then_inc(bank_free[s], 1)
            return
        (silu, both), steps = more
        j = s // 2
        if j == 0:
            steps.at(i * 4)
        eng.wait_ge(bank_free[s - 1], i + 2)
        nc.vector.tensor_tensor(both[:, :], ps[:, :], silu[j][:, :], ALU.mult).then_inc(bank_free[s], 1)
        eng.wait_ge(bank_free[s], i + 2)
        n = bass.ds(i * 2 + j, 1)
        steps.after(nc.vector.tensor_copy(flat(a_hi[:, n, :]), both[:, :]))
        steps.after(nc.vector.tensor_tensor(flat(a_lo[:, n, :]), both[:, :], flat(a_hi[:, n, :]).bitcast(F32),
                                            ALU.subtract))

    linear(nc, name, FC // 2, slots, ["act", "dve"] * 2, evac, extra)


def rope_queries_keys(nc, name, C, q, k, misc):
    rows, all_rows = slice(MLA_ROPE0, MLA_QK), slice(0, MLA_QK)
    N = MLA_HEADS + 1
    with Stage(nc, name) as st:
        by_cos = [st.sb(f"by_cos{j}", [P, SEQ]) for j in range(2)]
        by_sin = [st.sb(f"by_sin{j}", [P, SEQ]) for j in range(2)]
        turned = [st.ps(f"turned{j}", [P, SEQ]) for j in range(2)]
        turn_done, sin_done, cos_done, item_done, copied = (
            st.sem(x) for x in ("turn_done", "sin_done", "cos_done", "item_done", "copied"))
        tiles = [q[all_rows, h, :] for h in range(MLA_HEADS)] + [misc[all_rows, :]]
        with nc.Block() as block:

            @block.tensor
            def _(pe):
                for n, t in enumerate(tiles):
                    if n >= 2:
                        pe.wait_ge(sin_done, n - 1)
                    nc.tensor.matmul(turned[n % 2][all_rows, :], C.turn2[all_rows, 0:MLA_QK], t, start=True,
                                     stop=True).then_inc(turn_done, 1)

            @block.gpsimd
            def _(pool):
                for n, t in enumerate(tiles):
                    if n >= 2:
                        pool.wait_ge(item_done, n - 1)
                    nc.gpsimd.tensor_tensor(by_cos[n % 2][rows, :], t[rows, :], C.cos2[rows, :],
                                            ALU.mult).then_inc(cos_done, 1)

            @block.vector
            def _(dve):
                for n, t in enumerate(tiles):
                    dve.wait_ge(turn_done, n + 1)
                    if n >= 2:
                        dve.wait_ge(item_done, n - 1)
                    nc.vector.tensor_tensor(by_sin[n % 2][rows, :], turned[n % 2][rows, :], C.sin2[rows, :],
                                            ALU.mult).then_inc(sin_done, 1)
                    dve.wait_ge(sin_done, n + 1)
                    dve.wait_ge(cos_done, n + 1)
                    nc.vector.tensor_tensor(t[rows, :], by_cos[n % 2][rows, :], by_sin[n % 2][rows, :],
                                            ALU.add).then_inc(item_done, 1)

            @block.scalar
            def _(act):
                act.wait_ge(item_done, N)
                for h in range(MLA_HEADS):
                    nc.scalar.activation(k[rows, h, :], misc[rows, :], ACT.Copy)


CONST1 = (("ident", P), ("ones", P), ("iota", P), ("eps", 1), ("heads", P), ("turn", P), ("cos", SEQ), ("sin", SEQ),
          ("causal", P), ("cmp_add", TT * N_CMP), ("cmp_keep", TT * N_CMP), ("band", 4 * SEQ), ("every4", P))
CONST2 = (("ident", P), ("ones", P), ("eps", 1), ("cum", P), ("rev", P), ("same", P), ("inv_count", 4 * SEQ),
          ("turn2", P), ("inv_freq", 1), ("causal", P))
GAINS1 = (("norm1", DC), ("norm2", DC), ("q", 1), ("k0", 1), ("k1", 1), ("k2", 1), ("dq", 3), ("dk", 3))
GAINS2 = (("pre_mix", DC), ("post_mix", DC), ("pre_ffn", DC), ("post_ffn", DC), ("pool", 4), ("gla", 4),
          ("mla_q", 3), ("mla_kv", 2))


class Packed:

    def __init__(self, tile, layout):
        self.tile, self.at, col = tile, {}, 0
        for name, width in layout:
            self.at[name] = (col, col + width)
            col += width

    def __getitem__(self, name):
        return self.tile[:, self.at[name][0]:self.at[name][1]]


class Constants:
    pass


def width_of(layout):
    return sum(w for _, w in layout)


def np_constants():
    f = np.float32
    i = np.arange(P)
    t = np.arange(SEQ)
    out = {}
    out["ident"] = np.eye(P)
    out["ones"] = np.ones((P, P))
    out["iota"] = np.tile(i, (P, 1))
    out["eps"] = np.full((P, 1), EPS)
    out["heads"] = (i[:, None] // HD == i[None, :] // HD)
    turn = np.zeros((P, P))
    for b in (0, HD):
        for j in range(8):
            turn[b + 8 + j, b + j] = -1
            turn[b + j, b + 8 + j] = 1
    out["turn"] = turn
    inv = (f(500000.0) ** -(np.arange(8, dtype=f) * f(2.0) / f(16))).astype(f)
    ang = (t.astype(f)[None, :] * inv[:, None]).astype(np.float64)
    cos, sin = np.ones((P, SEQ)), np.zeros((P, SEQ))
    for b in (0, 8, HD, HD + 8):
        cos[b:b + 8], sin[b:b + 8] = np.cos(ang), np.sin(ang)
    out["cos"], out["sin"] = cos, sin
    out["causal"] = np.where(i[None, :] <= i[:, None], 0.0, NEG)
    ends = np.arange(N_CMP) * CMP_STRIDE + CMP_BLOCK - 1
    seen = np.stack([ends[None, :] <= (q * P + i)[:, None] for q in range(TT)], 1).reshape(P, -1)
    out["cmp_add"], out["cmp_keep"] = np.where(seen, 0.0, NEG), seen
    far = [(4 * i + r)[:, None] - t[None, :] for r in range(4)]
    out["band"] = np.concatenate([np.where((d >= 0) & (d <= 128), 0.0, NEG) for d in far], 1)
    d = i[:, None] - i[None, :]
    out["every4"] = np.where((d >= 0) & (d % 4 == 0), 0.0, NEG)
    chunk = i[:, None] // GLA_CHUNK == i[None, :] // GLA_CHUNK
    out["same"] = chunk & (i[:, None] <= i[None, :])
    out["cum"] = out["same"] / 16.0
    out["rev"] = (chunk & (i[:, None] > i[None, :])) / 16.0
    out["inv_count"] = np.tile(np.concatenate([1.0 / np.minimum(t + 1, w) for w in POOL_WINDOWS]), (P, 1))
    turn2 = np.zeros((P, P))
    for j in range(16):
        turn2[MLA_ROPE0 + 16 + j, MLA_ROPE0 + j] = -1
        turn2[MLA_ROPE0 + j, MLA_ROPE0 + 16 + j] = 1
    out["turn2"] = turn2
    freq = (f(10000.0) ** (-np.arange(0, 32, 2, dtype=f) / f(32))).astype(f)
    inv_freq = np.zeros((P, 1))
    inv_freq[MLA_ROPE0:MLA_QK, 0] = np.tile(freq, 2)
    out["inv_freq"] = inv_freq
    return out


def pack(parts, layout):
    return np.ascontiguousarray(np.concatenate([np.asarray(parts[n], np.float32).reshape(P, w) for n, w in layout], 1))


def by_partition(g):
    return g.reshape(-1, P).T


def lay_chunks(w, cols=None):
    if cols is not None:
        w = np.concatenate([w, np.zeros((w.shape[0], 1), w.dtype)], 1)[:, cols]
    K, N = w.shape
    return np.ascontiguousarray(w.reshape(K // P, P, N // P, P).transpose(2, 1, 0, 3).reshape(N // P, P, K))


def lay_rows(w):
    return np.ascontiguousarray(w.reshape(-1, P, w.shape[1]).transpose(1, 0, 2))


def layout(x):
    c, a = np_constants(), {}
    pair = [64 * h + j for n in range(NSA_PAIRS) for h in (n, n + NSA_PAIRS) for j in range(HD)]
    dil0 = 1304
    z_cols = pair + list(range(512, 896)) + list(range(1024, 1152))
    for g in range(3):
        z_cols += list(range(dil0 + 768 * g, dil0 + 768 * g + 512))
    z_cols += list(range(3608, 5656))
    v0, v1, v2 = (list(range(dil0 + 768 * g + 512, dil0 + 768 * g + 768)) for g in range(3))
    w = x["w_in"]
    a["x_t"] = np.ascontiguousarray(x["x"][0].T.reshape(DC, P, SEQ).transpose(1, 0, 2))
    a["const1"], a["const2"] = pack(c, CONST1), pack(c, CONST2)
    two = lambda g: np.concatenate([g, g], -1).reshape(-1, P).T
    a["gains1"] = pack({"norm1": by_partition(x["norm1_g"]), "norm2": by_partition(x["norm2_g"]),
                        "q": two(x["nsa_q_norm"]), "k0": two(x["nsa_k_norm"][0]), "k1": two(x["nsa_k_norm"][1]),
                        "k2": two(x["nsa_k_norm"][2]), "dq": two(x["dil_q_norm"]), "dk": two(x["dil_k_norm"])}, GAINS1)
    a["w_z"] = lay_chunks(w, z_cols)
    a["w_v"] = lay_rows(w[:, list(range(896, 1024)) + list(range(1152, 1280)) + v0])
    a["w_g"] = lay_rows(w[:, 1280:1304])
    a["w_v4"] = lay_rows(w[:, v1 + v2])
    for n in "kv":
        a[f"pe_{n}"] = np.ascontiguousarray(x[f"cmp_pe_{n}"].T)
        a[f"w1_{n}"], a[f"w2_{n}"] = x[f"cmp_w1_{n}"], x[f"cmp_w2_{n}"]
    a["w_up_nsa"] = lay_chunks(x["w_up_nsa"][pair])
    a["w_up_dil"], a["w_o"], a["w_q"] = lay_chunks(x["w_up_dil"]), lay_chunks(x["w_o"]), lay_chunks(x["peer_wq"])
    a["subkeys"] = np.ascontiguousarray(x["peer_subkeys"].transpose(0, 2, 1).reshape(P, KEYS))
    a["u"] = np.ascontiguousarray(x["peer_u"].reshape(KEYS, KEYS, DC, P).transpose(1, 3, 2, 0).reshape(KEYS, P, D))
    a["v"] = x["peer_v"]

    a["positions"] = x["positions_2"]
    empty = [-1]
    misc0 = 512 + 256 + 256 + 512 + 512
    y_cols = (list(range(0, 1024)) + list(range(1536, 2048)) + list(range(misc0 + 16, misc0 + 16 + 640))
              + list(range(misc0 + 16 + 640 + 32, misc0 + 16 + 640 + 32 + 3 * D))
              + list(range(misc0, misc0 + 16)) + empty * 48 + list(range(misc0 + 656, misc0 + 688)) + empty * 32)
    q_cols = [c for h in range(MLA_HEADS) for c in list(range(96 * h, 96 * h + 96)) + empty * 32]
    k_cols = [c for h in range(MLA_HEADS) for c in list(range(128 * h, 128 * h + 64)) + empty * 64]
    v_cols = [c for h in range(MLA_HEADS) for c in range(128 * h + 64, 128 * h + 128)]
    gu_cols = [c for n in range(FC) for s in (0, D_FF) for c in range(s + P * n, s + P * n + P)]
    each = lambda f: np.ascontiguousarray(np.stack([f(n) for n in range(LAYERS)]))
    all_of = lambda f: np.ascontiguousarray(np.concatenate([f(n) for n in range(LAYERS)]))
    a["gains2"] = each(lambda n: pack({
        "pre_mix": by_partition(x["norm_pre_mix_2"][n]), "post_mix": by_partition(x["norm_post_mix_2"][n]),
        "pre_ffn": by_partition(x["norm_pre_ffn_2"][n]), "post_ffn": by_partition(x["norm_post_ffn_2"][n]),
        "pool": by_partition(x["pool_scale_2"][n]), "gla": by_partition(x["gla_norm_2"][n]),
        "mla_q": by_partition(x["mla_q_norm_2"][n]), "mla_kv": by_partition(x["mla_kv_norm_2"][n])}, GAINS2))
    a["l_y"] = all_of(lambda n: lay_chunks(x["w_in_2"][n], y_cols))
    a["l_gv"] = each(lambda n: lay_rows(x["w_in_2"][n][:, 1024:1536]))
    a["l_pool"] = each(lambda n: x["w_pool_2"][n].transpose(1, 0, 2))
    a["l_a2"] = each(lambda n: np.concatenate([x["w_gla_a2_2"][n], x["b_gla_a_2"][n][None]]))
    a["l_uq"] = all_of(lambda n: lay_chunks(x["w_mla_uq_2"][n], q_cols))
    a["l_uk"] = all_of(lambda n: lay_chunks(x["w_mla_ukv_2"][n], k_cols))
    a["l_uv"] = each(lambda n: lay_rows(x["w_mla_ukv_2"][n][:, v_cols]))
    for to, of in (("l_wa", "w_a_2"), ("l_wb", "w_b_2"), ("l_wc", "w_c_2"), ("l_wo", "w_o_2"), ("l_down", "w_ffn_down_2")):
        a[to] = all_of(lambda n, of=of: lay_chunks(x[of][n]))
    a["l_gu"] = all_of(lambda n: lay_chunks(x["w_ffn_gu_2"][n], gu_cols))
    return a


def dilated(nc, C, view, z, v_tok, v4_tok, every4, y_dil, ahead):
    units = []
    for n in range(2):
        for half in range(2):
            rows = slice(64 * half, 64 * half + 64)
            for r, at in enumerate(every4):
                q = [z[rows, Z_DIL + 4 * g + n, at] for g in range(3)]
                k = [z[rows, Z_DIL + 4 * g + 2 + n, at if g else slice(0, SEQ)] for g in range(3)]
                units.append(Unit(
                    scores=[(0, SEQ, q[0], k[0], 0, SEQ, view["band"][:, r * SEQ:(r + 1) * SEQ]),
                            (512, P, q[1], k[1], 512, P, view["causal"]),
                            (640, P, q[2], k[2], 640, P, view["every4"])],
                    parts=[(0, 768, None, None)],
                    values=[(s * P, v_tok[:, s, 256 + n * P:256 + (n + 1) * P]) for s in range(TT)]
                    + [(512 + g * P, v4_tok[:, r, 256 * g + n * P:256 * g + (n + 1) * P]) for g in range(2)],
                    rows=rows, dst=y_dil[rows, n, at]))
    attention(nc, "dil", C, units, HD ** -0.5, 768, ahead)


def first_block(nc, A, x, w_dram):
    mem = Memory(nc)
    sb = mem.sb
    with mem.scope():
        const = sb("const1_sb", [P, width_of(CONST1)])
        gains_sb = sb("gains1_sb", [P, width_of(GAINS1)])
        view, gains = Packed(const, CONST1), Packed(gains_sb, GAINS1)
        C = Constants()
        C.ident, C.ones, C.iota, C.eps = view["ident"], view["ones"], view["iota"], view["eps"]
        load(nc, "const1_load", [(const[:, :], A["const1"]), (gains_sb[:, :], A["gains1"]), (x[:, :, :], A["x_t"])])

        with mem.scope():
            z = sb("z", [P, Z_CHUNKS, SEQ])
            v_tok, v4_tok, gates = sb("v_tok", [P, TT, SEQ]), sb("v4_tok", [P, 4, SEQ]), sb("gates", [P, TT, 24])
            tiles = [slice(t * P, (t + 1) * P) for t in range(TT)]
            every4 = [slice(r, SEQ, 4) for r in range(4)]
            with nc.sbuf_tensor("h1_hi", [P, DC, SEQ], F32R) as h_hi, nc.sbuf_tensor("h1_lo", [P, DC, SEQ], F32R) as h_lo:
                rms_norm(nc, "norm1", C, x, gains["norm1"], DC, hi=h_hi, lo=h_lo)
                with Stage(nc, "proj_v_load") as early:
                    raw, ahead = ahead_rows(early, "w_v", A["w_v"])
                    feature_major(nc, "proj1", Weights(A["w_z"], Z_CHUNKS), h_hi, h_lo, z, 2, ahead)
                    token_major(nc, "proj_v", h_hi, h_lo, [
                        (A["w_v"], tiles, [v_tok[:, t, :] for t in range(TT)]),
                        (A["w_v4"], every4, [v4_tok[:, r, :] for r in range(4)]),
                        (A["w_g"], tiles, [gates[:, t, :] for t in range(TT)])], raw, ahead)

            k_cmp, v_cmp = sb("k_cmp", [P, N_CMP]), sb("v_cmp", [P, P])

            def item(tile, gain, at=slice(0, SEQ)):
                return Item(tile, tile, gain=gain, group=view["heads"], cos=view["cos"][:, at],
                            sin=view["sin"][:, at], turn=view["turn"])

            items = [item(z[:, Z_Q + n, :], gains["q"]) for n in range(4)]
            items += [item(z[:, Z_KS, :], gains["k1"]), item(z[:, Z_KW, :], gains["k2"])]
            for g in range(3):
                for n in range(4):
                    both = gains["dq"] if n < 2 else gains["dk"]
                    items.append(item(z[:, Z_DIL + 4 * g + n, :], both[:, g:g + 1]))
            norm_rope(nc, "rope1", C, items)
            y_dil = sb("y_dil", [P, 2, SEQ])
            with Stage(nc, "cmp_load") as early:
                both = [Compressing(early, "k", z[:, Z_KC, :], A["pe_k"], A["w1_k"], A["w2_k"], k_cmp, True),
                        Compressing(early, "v", z[:, Z_VC, :], A["pe_v"], A["w1_v"], A["w2_v"], v_cmp, False)]
                ahead = Ahead(early, "cmp", both[0].loads + both[1].loads)
                dilated(nc, C, view, z, v_tok, v4_tok, every4, y_dil, ahead)
                compress(nc, "cmp", C, both, ahead, [flat(gates[:, :, :]), flat(z[:, Z_MERGE:Z_CHUNKS, :])])
            norm_rope(nc, "rope_cmp", C, [item(k_cmp[:, :], gains["k0"], slice(CMP_BLOCK - 1, SEQ, CMP_STRIDE))])

            y_nsa = sb("y_nsa", [P, 4, SEQ])
            units = []
            for n in range(NSA_PAIRS):
                for g in range(2):
                    rows, head = slice(64 * g, 64 * g + 64), g * NSA_PAIRS + n
                    for t in range(TT):
                        w, at = (t + 1) * P, slice(t * P, (t + 1) * P)
                        q = z[rows, Z_Q + n, at]
                        add = view["cmp_add"][:, t * N_CMP:(t + 1) * N_CMP]
                        keep = view["cmp_keep"][:, t * N_CMP:(t + 1) * N_CMP]
                        units.append(Unit(
                            scores=[(0, w, q, z[rows, Z_KS, 0:w], t * P, P, view["causal"]),
                                    (512, w, q, z[rows, Z_KW, 0:w], 512 + t * P, P, view["causal"]),
                                    (1024, N_CMP, q, k_cmp[rows, :], 1024, N_CMP, add)],
                            parts=[(1024, N_CMP, gates[:, t, 3 * head:3 * head + 3], keep), (0, w, None, None),
                                   (512, w, None, None)],
                            values=[(1024, v_cmp[:, :])] + [(b + s * P, v_tok[:, s, c:c + P]) for b, c in
                                                            ((0, 0), (512, P)) for s in range(t + 1)],
                            rows=rows, dst=y_nsa[rows, n, at]))
            attention(nc, "nsa", C, units, HD ** -0.5, 1024 + P)

            with mem.scope():
                m_hi, m_lo = sb("m1_hi", [P, DC, SEQ], F32R), sb("m1_lo", [P, DC, SEQ], F32R)
                with nc.sbuf_tensor("y1_hi", [P, 6, SEQ], F32R) as y_hi, nc.sbuf_tensor("y1_lo", [P, 6, SEQ], F32R) as y_lo:
                    split(nc, "split_y", [(y_nsa[:, n, :], y_hi[:, n, :], y_lo[:, n, :]) for n in range(4)]
                          + [(y_dil[:, n, :], y_hi[:, 4 + n, :], y_lo[:, 4 + n, :]) for n in range(2)])
                    gated_merge(nc, "up1", [Weights(A["w_up_nsa"], DC), Weights(A["w_up_dil"], DC)],
                                [(y_hi[:, 0:4, :], y_lo[:, 0:4, :]), (y_hi[:, 4:6, :], y_lo[:, 4:6, :])],
                                z[:, Z_MERGE:Z_CHUNKS, :], m_hi, m_lo)
                add_product(nc, "out1", Weights(A["w_o"], DC), m_hi, m_lo, x, 2)

        with mem.scope():
            h_hi, h_lo = sb("h2_hi", [P, DC, SEQ], F32R), sb("h2_lo", [P, DC, SEQ], F32R)
            rms_norm(nc, "norm2", C, x, gains["norm2"], DC, hi=h_hi, lo=h_lo)
            with nc.sbuf_tensor("chosen", [P, 3, SEQ], F32) as chosen:
                with nc.sbuf_tensor("peer_q", [P, DC, SEQ], F32) as q:
                    feature_major(nc, "peer_q_proj", Weights(A["w_q"], DC), h_hi, h_lo, q, 4)
                    expert_choice(nc, "choice", C, q, A["subkeys"], chosen)
                expert_weights(nc, "weights", C, chosen, w_dram)
            experts(nc, "experts", C, x, h_hi, h_lo, A["u"], A["v"], w_dram)


def second_block(nc, A, x):
    mem = Memory(nc)
    sb = mem.sb
    with mem.scope():
        const = sb("const2_sb", [P, width_of(CONST2)])
        gains_sb = sb("gains2_sb", [P, width_of(GAINS2)])
        view, gains = Packed(const, CONST2), Packed(gains_sb, GAINS2)
        C = Constants()
        C.ident, C.ones, C.eps, C.cum, C.rev, C.same = (view[n] for n in ("ident", "ones", "eps", "cum", "rev", "same"))
        C.turn2, C.inv_freq = view["turn2"], view["inv_freq"]
        C.inv_count = view["inv_count"].rearrange("p (g t) -> p g t", g=4)
        C.cos2, C.sin2 = sb("cos2", [P, SEQ]), sb("sin2", [P, SEQ])
        load(nc, "const2_load", [(const[:, :], A["const2"])])
        angles(nc, "angles", C, A["positions"])
        with nc.Fori(0, LAYERS) as layer:
            one_layer(nc, A, x, C, view, gains, gains_sb, layer)


def one_layer(nc, A, x, C, view, gains, gains_sb, layer):
    mem = Memory(nc)
    sb = mem.sb
    with mem.scope():
        def weights(name, n):
            return Weights(A[name], n, layer * n)

        def of_layer(name, spec):
            return A[name][bass.ds(layer, 1)].rearrange(spec)

        tiles = [slice(t * P, (t + 1) * P) for t in range(TT)]
        load(nc, "gains2_load", [(gains_sb[:, :], of_layer("gains2", "a p g -> p (a g)"))])
        with mem.scope():
            y, v_gla = sb("y", [P, Y_CHUNKS, SEQ]), sb("v_gla", [P, TT, SEQ])
            with nc.sbuf_tensor("h3_hi", [P, DC, SEQ], F32R) as h_hi, nc.sbuf_tensor("h3_lo", [P, DC, SEQ], F32R) as h_lo:
                rms_norm(nc, "pre_mix", C, x, gains["pre_mix"], DC, hi=h_hi, lo=h_lo)
                with Stage(nc, "proj_gv_load") as early:
                    w_gv = of_layer("l_gv", "a p k n -> p (a k) n")
                    raw, ahead = ahead_rows(early, "w_gv", w_gv)
                    feature_major(nc, "proj2", weights("l_y", Y_CHUNKS), h_hi, h_lo, y, 2, ahead)
                    token_major(nc, "proj_gv", h_hi, h_lo, [(w_gv, tiles, [v_gla[:, t, :] for t in range(TT)])],
                                raw, ahead)
            pool_mixer(nc, "pool", C, y[:, Y_POOL:Y_POOL + 4, :], of_layer("l_pool", "a p g m -> p (a g) m"), gains["pool"],
                       flat(y[:, Y_GATE:Y_MISC, :]))
            gla_mixer(nc, "gla", C, y, v_gla, of_layer("l_a2", "a r m -> (a r) m"), gains["gla"])
            with mem.scope():
                q, k, v_mla = sb("q2", [P, MLA_HEADS, SEQ]), sb("k2", [P, MLA_HEADS, SEQ]), sb("v2", [P, TT, SEQ])
                with nc.sbuf_tensor("c_hi", [P, 3, SEQ], F32R) as c_hi, nc.sbuf_tensor("c_lo", [P, 3, SEQ], F32R) as c_lo:
                    rms_norm(nc, "mla_q_norm", C, y[:, Y_CQ:Y_CQ + 3, :], gains["mla_q"], 3, hi=c_hi, lo=c_lo)
                    feature_major(nc, "mla_uq", weights("l_uq", MLA_HEADS), c_hi, c_lo, q, 4)
                with nc.sbuf_tensor("kv_hi", [P, 2, SEQ], F32R) as c_hi, nc.sbuf_tensor("kv_lo", [P, 2, SEQ], F32R) as c_lo:
                    rms_norm(nc, "mla_kv_norm", C, y[:, Y_CKV:Y_CKV + 2, :], gains["mla_kv"], 2, hi=c_hi, lo=c_lo)
                    feature_major(nc, "mla_uk", weights("l_uk", MLA_HEADS), c_hi, c_lo, k, 4)
                    token_major(nc, "mla_uv", c_hi, c_lo, [(of_layer("l_uv", "a p k n -> p (a k) n"), tiles,
                                                            [v_mla[:, t, :] for t in range(TT)])])
                rope_queries_keys(nc, "rope2", C, q, k, y[:, Y_MISC, :])
                units = []
                for h in range(MLA_HEADS):
                    for t in range(TT):
                        w, at = (t + 1) * P, slice(t * P, (t + 1) * P)
                        units.append(Unit(
                            scores=[(0, w, q[0:MLA_QK, h, at], k[0:MLA_QK, h, 0:w], t * P, P, view["causal"])],
                            parts=[(0, w, None, None)],
                            values=[(s * P, v_mla[:, s, P * (h // 2):P * (h // 2) + P]) for s in range(t + 1)],
                            rows=slice(64 * (h % 2), 64 * (h % 2) + 64), dst=y[64 * (h % 2):64 * (h % 2) + 64, Y_CQ + h // 2, at]))
                attention(nc, "mla", C, units, MLA_QK ** -0.5, SEQ)
            gates = y[:, Y_GATE:Y_MISC, :]
            with nc.sbuf_tensor("y_hi", [P, 12, SEQ], F32R) as y_hi, nc.sbuf_tensor("y_lo", [P, 12, SEQ], F32R) as y_lo:
                starts = (Y_POOL, Y_GR, Y_CQ)
                split(nc, "split_y2", [(y[:, s + n, :], y_hi[:, 4 * j + n, :], y_lo[:, 4 * j + n, :])
                                       for j, s in enumerate(starts) for n in range(4)])
                gated_merge(nc, "merge2", [weights(n, DC) for n in ("l_wa", "l_wb", "l_wc")],
                            [(y_hi[:, 4 * j:4 * j + 4, :], y_lo[:, 4 * j:4 * j + 4, :]) for j in range(3)], gates)
            m = sb("m2", [P, DC, SEQ])
            with nc.sbuf_tensor("m2_hi", [P, DC, SEQ], F32R) as m_hi, nc.sbuf_tensor("m2_lo", [P, DC, SEQ], F32R) as m_lo:
                split(nc, "split_m2", [(gates[:, n, :], m_hi[:, n, :], m_lo[:, n, :]) for n in range(DC)])
                feature_major(nc, "out2", weights("l_wo", DC), m_hi, m_lo, m, 2)
            rms_norm(nc, "post_mix", C, m, gains["post_mix"], DC, add_to=x)
        with mem.scope():
            a_hi, a_lo = sb("a2_hi", [P, FC, SEQ], F32R), sb("a2_lo", [P, FC, SEQ], F32R)
            with nc.sbuf_tensor("h4_hi", [P, DC, SEQ], F32R) as h_hi, nc.sbuf_tensor("h4_lo", [P, DC, SEQ], F32R) as h_lo:
                rms_norm(nc, "pre_ffn", C, x, gains["pre_ffn"], DC, hi=h_hi, lo=h_lo)
                gated_ffn(nc, "ffn_up", weights("l_gu", 2 * FC), h_hi, h_lo, a_hi, a_lo)
            f = sb("f2", [P, DC, SEQ])
            feature_major(nc, "ffn_down", weights("l_down", DC), a_hi, a_lo, f, 2)
            rms_norm(nc, "post_ffn", C, f, gains["post_ffn"], DC, add_to=x)


def store(nc, x, out):
    with Stage(nc, "store") as st:
        stored = st.sem("stored")
        with nc.Block() as block:

            @block.sync
            def _(sp):
                sp.dma_start(out, x[:, :, :]).then_inc(stored, 16)
                sp.wait_ge(stored, 16)


def program(nc, A, out):
    w_dram = nc.dram_tensor("expert_weights", [WTT, P, KEYS * WT], F32, kind="Internal").ap()
    with nc.sbuf_tensor("x_sb", [P, DC, SEQ], F32) as x:
        first_block(nc, A, x, w_dram)
        second_block(nc, A, x)
        store(nc, x, out)


def kernel(**inputs):
    import concourse.bacc as bacc
    from concourse.bass_utils import run_bass_kernel_spmd

    nc = bacc.Bacc("TRN2", target_bir_lowering=False, num_devices=1)
    arrays = layout({n: np.asarray(v) for n, v in inputs.items()})
    A = {n: nc.dram_tensor(n, a.shape, mybir.dt.from_np(a.dtype), kind="ExternalInput").ap() for n, a in arrays.items()}
    out = nc.dram_tensor("out_t", (P, DC, SEQ), F32, kind="ExternalOutput").ap()
    program(nc, A, out)
    got = run_bass_kernel_spmd(nc, [arrays], core_ids=[0]).results[0]["out_t"]
    return np.ascontiguousarray(got.transpose(2, 1, 0).reshape(1, SEQ, D))
```
